# Optimizing a Trainium2 kernel written in Bass

```python
import math
import jax
import jax.numpy as jnp
from jax import lax
import numpy as np

D_MODEL = 2048
BATCH = 1
SEQ = 256
DEPTH = 2

ROPE_THETA = 10000.0
RMS_EPS = 1e-6
DIFF_SUBLN_EPS = 1e-5
A_HEAD_DIM = 128
A_HEADS = D_MODEL // 256
A_WIDTH = A_HEADS * A_HEAD_DIM
MOBA_BLOCK = 256
MOBA_TOPK = 3
MOBA_Q_CHUNK = 64
B_HEAD_DIM = 128
B_HEADS = D_MODEL // 512
B_WIDTH = 2 * B_HEADS * B_HEAD_DIM
DENSE_Q_BLOCK = 128
EVEN_IN = 3 * A_WIDTH + 3 * B_WIDTH
EVEN_OUT = A_WIDTH + B_WIDTH
C_HEAD_DIM = 64
C_Q_HEADS = D_MODEL // C_HEAD_DIM
C_KV_HEADS = C_Q_HEADS // 8
C_WINDOW = 128
C_Q_WIDTH = C_Q_HEADS * C_HEAD_DIM
C_KV_WIDTH = C_KV_HEADS * C_HEAD_DIM
ODD_IN = C_Q_WIDTH + 2 * C_KV_WIDTH
FFN_HIDDEN = -(-8 * D_MODEL // (3 * 256)) * 256
N_EVEN = (DEPTH + 1) // 2
N_ODD = DEPTH // 2
N_MOD = 6

kernel_name = "hybrid_moba_diff_swa_adaln_trunk"

def rms_norm(x, w=None, eps=RMS_EPS):
    xf = x.astype(jnp.float32)
    y = xf * lax.rsqrt(jnp.mean(xf * xf, axis=-1, keepdims=True) + eps)
    if w is not None:
        y = y * w.astype(jnp.float32)
    return y.astype(x.dtype)

def rope_tables(seq, dim):
    pos = jnp.arange(seq, dtype=jnp.float32)
    inv_freq = ROPE_THETA ** (-jnp.arange(0, dim, 2, dtype=jnp.float32) / dim)
    ang = pos[:, None] * inv_freq[None, :]
    return jnp.cos(ang), jnp.sin(ang)

def apply_rope(x, cos, sin):
    xf = x.astype(jnp.float32)
    half = xf.shape[-1] // 2
    x1, x2 = xf[..., :half], xf[..., half:]
    out = jnp.concatenate([x1 * cos - x2 * sin, x2 * cos + x1 * sin], axis=-1)
    return out.astype(x.dtype)

def split_heads(t, n_heads, head_dim):
    bsz, seq, _ = t.shape
    return t.reshape(bsz, seq, n_heads, head_dim).transpose(0, 2, 1, 3)

def merge_heads(t):
    bsz, nh, seq, dh = t.shape
    return t.transpose(0, 2, 1, 3).reshape(bsz, seq, nh * dh)

def lambda_init_fn(layer):
    return 0.8 - 0.6 * math.exp(-0.3 * layer)

def moba_attention(q, k, v):
    bsz, nh, seq, dh = q.shape
    nb = -(-seq // MOBA_BLOCK)
    padded = nb * MOBA_BLOCK
    if padded != seq:
        pad = ((0, 0), (0, 0), (0, padded - seq), (0, 0))
        q, k, v = jnp.pad(q, pad), jnp.pad(k, pad), jnp.pad(v, pad)
    topk = min(MOBA_TOPK, nb)
    n_chunks = padded // MOBA_Q_CHUNK
    scale = dh ** -0.5
    kb = k.reshape(bsz, nh, nb, MOBA_BLOCK, dh)
    vb = v.reshape(bsz, nh, nb, MOBA_BLOCK, dh)
    k_mean = jnp.mean(kb.astype(jnp.float32), axis=3)
    q_chunks = jnp.moveaxis(q.reshape(bsz, nh, n_chunks, MOBA_Q_CHUNK, dh), 2, 0)
    b_idx = jnp.arange(bsz)[:, None, None, None]
    h_idx = jnp.arange(nh)[None, :, None, None]
    blk_ids = jnp.arange(nb)
    q_offs = jnp.arange(MOBA_Q_CHUNK)
    k_offs = jnp.arange(MOBA_BLOCK)

    def one_chunk(args):
        qi, ci = args
        q_pos = ci * MOBA_Q_CHUNK + q_offs
        own = (ci * MOBA_Q_CHUNK) // MOBA_BLOCK
        gate = jnp.einsum('bhqd,bhnd->bhqn', qi.astype(jnp.float32), k_mean)
        gate = jnp.where(blk_ids < own, gate, -jnp.inf)
        _, sel = lax.top_k(gate, topk)
        sel_valid = sel < own
        k_sel = kb[b_idx, h_idx, sel]
        v_sel = vb[b_idx, h_idx, sel]
        s_sel = jnp.einsum('bhqd,bhqjkd->bhqjk', qi, k_sel).astype(jnp.float32) * scale
        s_sel = jnp.where(sel_valid[..., None], s_sel, -jnp.inf)
        k_own = lax.dynamic_index_in_dim(kb, own, axis=2, keepdims=False)
        v_own = lax.dynamic_index_in_dim(vb, own, axis=2, keepdims=False)
        s_own = jnp.einsum('bhqd,bhkd->bhqk', qi, k_own).astype(jnp.float32) * scale
        k_pos = own * MOBA_BLOCK + k_offs
        s_own = jnp.where(k_pos[None, :] <= q_pos[:, None], s_own, -jnp.inf)
        logits = jnp.concatenate(
            [s_sel.reshape(bsz, nh, MOBA_Q_CHUNK, topk * MOBA_BLOCK), s_own], axis=-1)
        p = jax.nn.softmax(logits, axis=-1).astype(v.dtype)
        p_sel = p[..., :topk * MOBA_BLOCK].reshape(bsz, nh, MOBA_Q_CHUNK, topk, MOBA_BLOCK)
        p_own = p[..., topk * MOBA_BLOCK:]
        return (jnp.einsum('bhqjk,bhqjkd->bhqd', p_sel, v_sel)
                + jnp.einsum('bhqk,bhkd->bhqd', p_own, v_own))

    out = lax.map(one_chunk, (q_chunks, jnp.arange(n_chunks)))
    out = jnp.moveaxis(out, 0, 2).reshape(bsz, nh, padded, dh)
    return out[:, :, :seq]

def diff_attention(q, k, v, lam):
    bsz, n2, seq, dh = q.shape
    nh = n2 // 2
    n_blocks = seq // DENSE_Q_BLOCK
    scale = dh ** -0.5
    k_pos = jnp.arange(seq)
    q_offs = jnp.arange(DENSE_Q_BLOCK)
    q_blocks = jnp.moveaxis(q.reshape(bsz, n2, n_blocks, DENSE_Q_BLOCK, dh), 2, 0)

    def one_block(args):
        qi, bi = args
        q_pos = bi * DENSE_Q_BLOCK + q_offs
        s = jnp.einsum('bhqd,bhkd->bhqk', qi, k).astype(jnp.float32) * scale
        s = jnp.where(k_pos[None, :] <= q_pos[:, None], s, -jnp.inf)
        p = jax.nn.softmax(s, axis=-1).reshape(bsz, nh, 2, DENSE_Q_BLOCK, seq)
        w = (p[:, :, 0] - lam * p[:, :, 1]).astype(v.dtype)
        return jnp.einsum('bhqk,bhkd->bhqd', w, v)

    out = lax.map(one_block, (q_blocks, jnp.arange(n_blocks)))
    return jnp.moveaxis(out, 0, 2).reshape(bsz, nh, seq, v.shape[-1])

def sliding_window_sink_attention(q, k, v, sinks):
    bsz, n_q, seq, dh = q.shape
    n_kv = k.shape[1]
    grp = n_q // n_kv
    n_blocks = seq // C_WINDOW
    scale = dh ** -0.5
    pad = ((0, 0), (0, 0), (C_WINDOW, 0), (0, 0))
    kp, vp = jnp.pad(k, pad), jnp.pad(v, pad)
    q_blocks = jnp.moveaxis(q.reshape(bsz, n_kv, grp, n_blocks, C_WINDOW, dh), 3, 0)
    sink_logits = sinks.astype(jnp.float32).reshape(1, n_kv, grp, 1, 1)
    q_offs = jnp.arange(C_WINDOW)
    k_offs = jnp.arange(2 * C_WINDOW)

    def one_block(args):
        qi, bi = args
        kw = lax.dynamic_slice_in_dim(kp, bi * C_WINDOW, 2 * C_WINDOW, axis=2)
        vw = lax.dynamic_slice_in_dim(vp, bi * C_WINDOW, 2 * C_WINDOW, axis=2)
        q_pos = bi * C_WINDOW + q_offs
        k_pos = (bi - 1) * C_WINDOW + k_offs
        rel = q_pos[:, None] - k_pos[None, :]
        mask = (rel >= 0) & (rel < C_WINDOW) & (k_pos[None, :] >= 0)
        s = jnp.einsum('bkgqd,bksd->bkgqs', qi, kw).astype(jnp.float32) * scale
        s = jnp.where(mask, s, -jnp.inf)
        sink = jnp.broadcast_to(sink_logits, s.shape[:-1] + (1,))
        p = jax.nn.softmax(jnp.concatenate([s, sink], axis=-1), axis=-1)[..., :-1]
        return jnp.einsum('bkgqs,bksd->bkgqd', p.astype(v.dtype), vw)

    out = lax.map(one_block, (q_blocks, jnp.arange(n_blocks)))
    return jnp.moveaxis(out, 0, 3).reshape(bsz, n_q, seq, dh)

def even_mixer(h, w_in, w_out, lam_vecs, subln_w, lambda_init, cos_r, sin_r):
    proj = h @ w_in
    splits = [A_WIDTH, 2 * A_WIDTH, 3 * A_WIDTH,
              3 * A_WIDTH + B_WIDTH, 3 * A_WIDTH + 2 * B_WIDTH]
    aq, ak, av, bq, bk, bv = jnp.split(proj, splits, axis=-1)
    aq = apply_rope(split_heads(aq, A_HEADS, A_HEAD_DIM), cos_r, sin_r)
    ak = apply_rope(split_heads(ak, A_HEADS, A_HEAD_DIM), cos_r, sin_r)
    av = split_heads(av, A_HEADS, A_HEAD_DIM)
    ya = moba_attention(aq, ak, av)
    bq = apply_rope(split_heads(bq, 2 * B_HEADS, B_HEAD_DIM), cos_r, sin_r)
    bk = apply_rope(split_heads(bk, 2 * B_HEADS, B_HEAD_DIM), cos_r, sin_r)
    bv = split_heads(bv, B_HEADS, 2 * B_HEAD_DIM)
    lv = lam_vecs.astype(jnp.float32)
    lam = (jnp.exp(jnp.sum(lv[0] * lv[1])) - jnp.exp(jnp.sum(lv[2] * lv[3]))
           + lambda_init)
    yb = diff_attention(bq, bk, bv, lam)
    yb = rms_norm(yb, subln_w, DIFF_SUBLN_EPS) * (1.0 - lambda_init)
    y = jnp.concatenate([merge_heads(ya), merge_heads(yb)], axis=-1)
    return y @ w_out

def odd_mixer(h, w_in, b_in, w_out, b_out, sinks, cos_r, sin_r):
    proj = h @ w_in + b_in
    q, k, v = jnp.split(proj, [C_Q_WIDTH, C_Q_WIDTH + C_KV_WIDTH], axis=-1)
    q = apply_rope(split_heads(q, C_Q_HEADS, C_HEAD_DIM), cos_r, sin_r)
    k = apply_rope(split_heads(k, C_KV_HEADS, C_HEAD_DIM), cos_r, sin_r)
    v = split_heads(v, C_KV_HEADS, C_HEAD_DIM)
    y = sliding_window_sink_attention(q, k, v, sinks)
    return merge_heads(y) @ w_out + b_out

def swiglu(h, w_in, w_out):
    gate, up = jnp.split(h @ w_in, 2, axis=-1)
    return (jax.nn.silu(gate) * up) @ w_out

def setup_inputs(seed: int = 0) -> dict:
    key = jax.random.key(seed)
    ks = jax.random.split(key, 17)

    def nrm(k, shape, s):
        return jax.random.normal(k, shape, jnp.float32) * s

    return {
        "x": nrm(ks[0], (BATCH, SEQ, D_MODEL), 1.0),
        "c": nrm(ks[1], (BATCH, D_MODEL), 1.0),
        "ada_w": nrm(ks[2], (DEPTH, D_MODEL, N_MOD * D_MODEL), 0.5 * D_MODEL ** -0.5),
        "ada_b": nrm(ks[3], (DEPTH, N_MOD * D_MODEL), 0.02),
        "ab_w_in": nrm(ks[4], (N_EVEN, D_MODEL, EVEN_IN), D_MODEL ** -0.5),
        "ab_w_out": nrm(ks[5], (N_EVEN, EVEN_OUT, D_MODEL), EVEN_OUT ** -0.5),
        "diff_lambda": nrm(ks[6], (N_EVEN, 4, B_HEAD_DIM), 0.1),
        "diff_subln": 1.0 + nrm(ks[7], (N_EVEN, 2 * B_HEAD_DIM), 0.02),
        "swa_w_in": nrm(ks[8], (N_ODD, D_MODEL, ODD_IN), D_MODEL ** -0.5),
        "swa_b_in": nrm(ks[9], (N_ODD, ODD_IN), 0.02),
        "swa_w_out": nrm(ks[10], (N_ODD, C_Q_WIDTH, D_MODEL), C_Q_WIDTH ** -0.5),
        "swa_b_out": nrm(ks[11], (N_ODD, D_MODEL), 0.02),
        "swa_sinks": nrm(ks[12], (N_ODD, C_Q_HEADS), 0.5),
        "ffn_w_in": nrm(ks[13], (DEPTH, D_MODEL, 2 * FFN_HIDDEN), D_MODEL ** -0.5),
        "ffn_w_out": nrm(ks[14], (DEPTH, FFN_HIDDEN, D_MODEL), FFN_HIDDEN ** -0.5),
        "final_norm": 1.0 + nrm(ks[15], (D_MODEL,), 0.02),
    }

def reference(x, c, ada_w, ada_b, ab_w_in, ab_w_out, diff_lambda, diff_subln,
              swa_w_in, swa_b_in, swa_w_out, swa_b_out, swa_sinks,
              ffn_w_in, ffn_w_out, final_norm):
    seq = x.shape[1]
    cos_ab, sin_ab = rope_tables(seq, A_HEAD_DIM)
    cos_c, sin_c = rope_tables(seq, C_HEAD_DIM)
    cond = jax.nn.silu(c.astype(jnp.float32)).astype(x.dtype)
    for layer in range(DEPTH):
        mod = cond @ ada_w[layer] + ada_b[layer]
        sh1, sc1, g1, sh2, sc2, g2 = jnp.split(mod[:, None, :], N_MOD, axis=-1)
        h = rms_norm(x) * (1.0 + sc1) + sh1
        i = layer // 2
        if layer % 2 == 0:
            y = even_mixer(h, ab_w_in[i], ab_w_out[i], diff_lambda[i], diff_subln[i],
                           lambda_init_fn(layer), cos_ab, sin_ab)
        else:
            y = odd_mixer(h, swa_w_in[i], swa_b_in[i], swa_w_out[i], swa_b_out[i],
                          swa_sinks[i], cos_c, sin_c)
        x = x + g1 * y
        h = rms_norm(x) * (1.0 + sc2) + sh2
        x = x + g2 * swiglu(h, ffn_w_in[layer], ffn_w_out[layer])
    return rms_norm(x, final_norm)


_drawn_inputs = setup_inputs


def setup_inputs(seed=0):
    import zlib

    import numpy as np

    out = dict(_drawn_inputs(seed))
    spreads = {}
    factors = {'diff_subln': 8.0,
     'swa_b_in': 8.0,
     'swa_b_out': 8.0,
     'swa_sinks': 8.0,
     'final_norm': 2.741}
    for name, (base, spread) in spreads.items():
        noise = np.random.default_rng([zlib.crc32(name.encode()), seed]).standard_normal(out[name].shape)
        drawn = base * np.exp(spread * noise) if base else spread * noise
        out[name] = jnp.asarray(drawn.astype(out[name].dtype))
    for name, factor in factors.items():
        out[name] = (out[name] * factor).astype(out[name].dtype)
    return out
```

```python
from contextlib import ExitStack

import numpy as np

import concourse.bass as bass
from concourse import mybir

ALU = mybir.AluOpType
ACT = mybir.ActivationFunctionType
F32 = mybir.dt.float32
F32R = mybir.dt.float32r
BF16 = mybir.dt.bfloat16
AX_X = mybir.AxisListType.X
ds = bass.ds

P = 128
D = 2048
SEQ = 256
TT = SEQ // P
NT = 512
KT = D // P
NB = D // NT
HID = 5632
HB = 256
ADA_COLS = 6 * D
RAW = 4
PAIRS = 4
ADA_RAW = 2
ACC = 8
SPLITS = (16, 16, 12)
LAMBDA_INIT = 0.2
RMS_EPS = 1e-6
SUBLN_EPS = 1e-5
MASKED = -1e30

LO_CREDIT = 2 * RAW
USED_CREDIT = PAIRS
ADA_CREDIT = 4 * ADA_RAW
ACC_CREDIT = ACC
EVAC_CREDIT = 2
HT_CREDIT = 2


class Phase:

    def __init__(self, prev, n, blocks, pairs, ada, src=None, src0=0):
        self.n, self.blocks, self.pairs, self.ada = n, blocks, pairs, ada
        self.quads = blocks * pairs // 2
        self.src, self.src0 = src, src0
        self.quad0 = prev.quad0 + prev.n * prev.quads if prev else 0
        self.block0 = prev.block0 + prev.n * prev.blocks if prev else 0
        self.ada0 = prev.ada0 + prev.n * prev.ada if prev else 0
        self.fills = [len(range(s, self.quads, RAW)) for s in range(RAW)]
        self.fills0 = [a + prev.n * b for a, b in zip(prev.fills0, prev.fills)] if prev else [0] * RAW

    def quad(self, i, t):
        return self.quad0 + i * self.quads + t

    def pair(self, i, p):
        return 2 * self.quad0 + i * (2 * self.quads) + p

    def block(self, i, b):
        return self.block0 + i * self.blocks + b

    def ada_quad(self, i, a):
        return 4 * self.ada0 + i * (4 * self.ada) + a

    def raw_fills(self, i, t):
        s = t % RAW
        return self.fills0[s] + i * self.fills[s] + t // RAW + 1

    def raw_distance(self, t):
        if t >= RAW or self.quads % RAW == 0:
            return RAW
        last = max(u for u in range(self.quads) if u % RAW == t % RAW)
        return self.quads - last + t

    def used(self, i, b):
        return USED_CREDIT + self.pair(i, (b + 1) * self.pairs)

    def ada_fills(self, i, a):
        return 2 * self.ada0 + i * (2 * self.ada) + a // ADA_RAW + 1

    def ada_after(self, t):
        n = 4 * self.ada
        return range(n * t // self.quads, n * (t + 1) // self.quads)


SH1, SC1, G1, SH2, SC2, G2 = (0, 6), (1, 7), (2, 9), (3, 8), (4, 10), (5, 11)
SUMMED_AT = (2, 5, 8, 11)


def heads_before(u, kind):
    return {"A": 4 * u, "B": 2 * u + 4, "C": 4 * u - 4}[kind]


def kernel_program(nc, T):
    chain = []

    def phase(*a, **k):
        chain.append(Phase(chain[-1] if chain else None, *a, **k))
        return chain[-1]

    MOD0 = phase(8, 0, 0, 1)
    AB_IN = phase(4, 3, 8, 2, src="ab_in")
    AB_OUT = phase(2, 2, 8, 2, src="ab_out")
    FFN = []
    C_KV = C_Q = C_OUT = None
    for layer in range(2):
        at_in, at_out, runs = layer * (HID // HB) * 4, layer * (HID // P), []
        for s, kts in enumerate(SPLITS):
            more = (layer == 0) or s == 0
            runs.append((phase(kts // 4, 2, 8, int(more), src="ffn_in", src0=at_in),
                         phase(2, 2, kts // 2, 2 * int(layer == 0 and s < 2), src="ffn_out", src0=at_out)))
            at_in += kts // 2 * 4
            at_out += kts
        FFN.append(runs)
        if layer == 0:
            C_KV = phase(1, 1, 8, 1, src="swa_in")
            C_Q = phase(2, 2, 8, 0, src="swa_in", src0=4)
            C_OUT = phase(2, 2, 8, 2, src="swa_out")
    assert chain[-1].ada0 == 48

    with ExitStack() as ctx:
        def sb(name, shape, dt=F32):
            return ctx.enter_context(nc.sbuf_tensor(name, shape, dt))

        def sem(name):
            return ctx.enter_context(nc.semaphore(name))

        x = sb("x", [P, TT, D])
        xT_hi = sb("xT_hi", [P, KT, SEQ], F32R)
        xT_lo = sb("xT_lo", [P, KT, SEQ], F32R)
        hT_hi = sb("hT_hi", [P, KT, SEQ], F32R)
        hT_lo = sb("hT_lo", [P, KT, SEQ], F32R)
        raw = sb("raw", [P, RAW, 4, NT])
        w_hi = sb("w_hi", [P, PAIRS, 2, NT], F32R)
        w_lo = sb("w_lo", [P, PAIRS, 2, NT], F32R)
        ada_raw = sb("ada_raw", [P, ADA_RAW, 4, NT])
        acc = sb("acc", [P, ACC, NT])
        work = sb("work", [P, 4096])
        gate = sb("gate", [P, D])
        ident = sb("ident", [P, P])
        ones = sb("ones", [P, P])
        ident_b = sb("ident_b", [P, P], BF16)
        mask_own = sb("mask_own", [P, P], BF16)
        mask_prev = sb("mask_prev", [P, P], BF16)
        rope_ab = sb("rope_ab", [P, TT, 2, 128])
        rope_c = sb("rope_c", [P, TT, 2, 64])
        subln = sb("subln", [P, 256])
        sinks = sb("sinks", [P, 32])
        cond = sb("cond", [P, KT])
        ada_bias = sb("ada_bias", [P, 2, 6, KT])
        mod = sb("mod", [P, 2, KT])
        ssq = sb("ssq", [P, 8])
        rstd = sb("rstd", [P, 8])
        top = sb("top", [P, TT, 4])
        negtop = sb("negtop", [P, TT, 4])
        den = sb("den", [P, TT, 4])
        rden = sb("rden", [P, TT, 4])
        sinkd = sb("sinkd", [P, TT, 4])
        sinke = sb("sinke", [P, TT, 4])
        lam = sb("lam", [P, 4])

        ps = ctx.enter_context(nc.psum_tensor("ps", [P, 8 * 512], F32))

        def bank(b, n=1):
            return ps[:, b * 512:(b + n) * 512]

        nat = work[:, 0:1024].rearrange("p (t n) -> p t n", t=TT)
        qT = work[:, 1024:2048].rearrange("p (h s) -> p h s", h=4)
        y = work[:, 1024:2048].rearrange("p (t n) -> p t n", t=TT)
        kT = work[:, 2048:3072].rearrange("p (h s) -> p h s", h=4)
        v_ab = work[:, 3072:4096].rearrange("p (t n) -> p t n", t=TT)
        q_c = v_ab
        k_c = work[:, 0:2048].rearrange("p (t g e n) -> p t g e n", t=TT, g=4, e=2)
        bias_c = work[:, 2048:2560]
        probs = gate[:, 0:1536].rearrange("p (h n) -> p h n", h=4)
        rope_t = gate[:, 1536:2048]
        kT_c = ada_raw[:, 0, :, :].rearrange("p a n -> p (a n)").rearrange("p (g s) -> p g s", g=8)
        v_c = ada_raw[:, 1, 0, :].rearrange("p (t n) -> p t n", t=TT)
        silu = work[:, 0:1024].rearrange("p (b t n) -> p b t n", b=2, t=TT)
        hid = work[:, 1024:2048].rearrange("p (b t n) -> p b t n", b=2, t=TT)
        upd = work[:, 2048:3072].rearrange("p (t n) -> p t n", t=TT)
        bias_o = work[:, 3072:4096].rearrange("p (b n) -> p b n", b=2)
        xn = work[:, :].rearrange("p (t n) -> p t n", t=TT)

        s_x = sem("x_landed")
        s_const = sem("constants_landed")
        s_cond = sem("cond_landed")
        raw_landed = [sem(f"raw_landed{s}") for s in range(RAW)]
        ada_landed = [sem(f"ada_landed{s}") for s in range(ADA_RAW)]
        gate_landed = sem("gate_row_landed")
        bias_landed = sem("c_bias_landed")
        bo_landed = [sem(f"c_out_bias_landed{s}") for s in range(2)]
        hi_ready = sem("hi_ready")
        lo_ready = sem("lo_ready")
        pair_used = sem("pair_used")
        evacuated = sem("evacuated")
        s_setup = sem("setup_done")
        s_silu_c = sem("silu_c_done")
        ada_step = sem("ada_step")
        mods_summed = sem("mods_summed")
        acc_free = sem("acc_free")
        ssq_done = sem("ssq_done")
        ms_done = sem("mean_square_done")
        root_done = sem("root_done")
        xn_done = sem("xn_done")
        xT_done = sem("xT_done")
        mod_act = sem("modulated_act")
        mod_dve = sem("modulated_dve")
        xh_done = sem("xT_hi_done")
        xl_done = sem("xT_lo_done")
        silu_done = sem("silu_done")
        hidT_done = sem("hidT_done")
        hTh_done = sem("hT_hi_done")
        hTl_done = sem("hT_lo_done")
        roped = sem("roped")
        qT_done = sem("qT_done")
        qT_copied = sem("qT_copied")
        kT_done = sem("kT_done")
        kT_copied = sem("kT_copied")
        scores_done = sem("scores_done")
        top_done = sem("top_done")
        probs_done = sem("probs_done")
        w_done = sem("w_done")
        pT_done = sem("pT_done")
        pT_act = sem("pT_copied_act")
        pT_dve = sem("pT_copied_dve")
        o_done = sem("o_done")
        sub_sq = sem("subln_square_done")
        sub_ms = sem("subln_mean_done")
        sub_root = sem("subln_root_done")
        y_done = sem("y_done")
        yT_done = sem("yT_done")
        yTh_done = sem("yT_hi_done")
        yTl_done = sem("yT_lo_done")
        out_landed = sem("out_landed")

        CONSTS = 8
        block = ctx.enter_context(nc.Block())

        def repeat(eng, lo, hi, body):
            if hi - lo == 1:
                body(lo)
            elif hi > lo:
                with eng.Fori(lo, hi) as i:
                    body(i)

        @block.sync
        def _(sp):
            sp.dma_start(cond[:, :], T["c"]).then_inc(s_cond, 16)

            def ada(ph, i, a):
                q = ph.ada_quad(i, a)
                sp.wait_ge(ada_step, 4 * q + 4)
                sp.dma_start(ada_raw[:, a % ADA_RAW, :, :].rearrange("p a n -> p (a n)"),
                             T["ada"][q]).then_inc(ada_landed[a % ADA_RAW], 16)

            def body(ph, i):
                for t in range(ph.quads):
                    sp.wait_ge(lo_ready, LO_CREDIT + 2 * (ph.quad(i, t) - ph.raw_distance(t) + 1))
                    sp.dma_start(raw[:, t % RAW, :, :].rearrange("p a n -> p (a n)"),
                                 T[ph.src][ph.src0 + i * ph.quads + t]).then_inc(raw_landed[t % RAW], 16)
                    for a in ph.ada_after(t):
                        if ph is C_OUT and a == 0 and isinstance(i, int):
                            sp.wait_ge(o_done, 12)
                        ada(ph, i, a)

            def mod0(i):
                for a in range(4):
                    ada(MOD0, i, a)
            repeat(sp, 0, 1, mod0)
            sp.dma_start(x[:, :, :], T["x"]).then_inc(s_x, 16)
            repeat(sp, 1, MOD0.n, mod0)
            for n, ph in enumerate(chain[1:]):
                if chain[n].quads % RAW:
                    sp.wait_ge(lo_ready, LO_CREDIT + 2 * ph.quad0)
                repeat(sp, 0, 1, lambda i: body(ph, i))
                repeat(sp, 1, ph.n, lambda i: body(ph, i))

            sp.wait_ge(xn_done, 10)
            sp.dma_start(T["out"], xn).then_inc(out_landed, 16)
            sp.wait_ge(out_landed, 16)

        @block.gpsimd
        def _(pool):
            pool.sem_inc(lo_ready, LO_CREDIT)
            pool.sem_inc(pair_used, USED_CREDIT)
            pool.sem_inc(ada_step, ADA_CREDIT)
            pool.sem_inc(acc_free, ACC_CREDIT)
            pool.sem_inc(evacuated, EVAC_CREDIT)
            pool.sem_inc(hidT_done, HT_CREDIT)
            pool.sem_inc(hTl_done, HT_CREDIT)
            pool.memset(ones[:, :], 1.0).then_inc(s_setup, 2)
            for dst, name in ((ident[:, :], "ident"), (rope_ab[:, :, :, :], "rope_ab"), (rope_c[:, :, :, :], "rope_c"),
                              (ada_bias[:, :, :, :], "ada_bias"), (work[:, 0:256], "masks")):
                pool.dma_start(dst, T[name]).then_inc(s_const, 16)
            for dst, name in ((subln[:, :], "subln"), (sinks[:, :], "sinks"), (work[:, 256:768], "lam")):
                pool.dma_start(dst, T[name].partition_broadcast(P)).then_inc(s_const, 16)

            def row(src):
                pool.dma_start(gate[:, :], src.partition_broadcast(P)).then_inc(gate_landed, 16)

            pool.wait_ge(o_done, 4)
            row(T["gate_bias"][0])
            pool.wait_ge(evacuated, EVAC_CREDIT + FFN[0][0][0].block0)
            row(T["gate_bias"][1])
            for c in range(5):
                if c == 0:
                    pool.wait_ge(xT_done, 12)
                else:
                    pool.wait_ge(evacuated, EVAC_CREDIT + C_KV.block0 + c)
                pool.dma_start(bias_c, T["swa_b_in"][c].partition_broadcast(P)).then_inc(bias_landed, 16)
            pool.wait_ge(o_done, 12)
            row(T["gate_bias"][2])
            pool.wait_ge(yT_done, 12)
            for n in range(NB):
                pool.wait_ge(evacuated, C_OUT.block(0, n) + 1)
                pool.dma_start(bias_o[:, n % 2, :],
                               T["swa_b_out"][n].partition_broadcast(P)).then_inc(bo_landed[n % 2], 16)
            pool.wait_ge(evacuated, EVAC_CREDIT + FFN[1][0][0].block0)
            row(T["gate_bias"][3])
            pool.wait_ge(evacuated, EVAC_CREDIT + chain[-1].block0 + 4)
            row(T["final_norm"])

        @block.scalar
        def _(act):
            def hi(ph, i, p):
                t = p // 2
                if p % 2 == 0:
                    act.wait_ge(raw_landed[t % RAW], 16 * ph.raw_fills(i, t))
                act.wait_ge(pair_used, ph.pair(i, p) + 1)
                nc.scalar.activation(w_hi[:, p % PAIRS, :, :], raw[:, t % RAW, 2 * (p % 2):2 * (p % 2) + 2, :],
                                     ACT.Copy).then_inc(hi_ready, 1)

            def norm(n, x_ready, ready):
                act.wait_ge(x_ready, ready)
                for t in range(TT):
                    last = nc.scalar.activation(xn[:, t, :], x[:, t, :], ACT.Square, accum_out=ssq[:, t:t + 1])
                last.then_inc(ssq_done, 1)
                act.wait_ge(ms_done, n + 1)
                nc.scalar.activation(rstd[:, 2:4], ssq[:, 2:4], ACT.Sqrt).then_inc(root_done, 1)

            def norm_out(n):
                def modulate(c):
                    act.wait_ge(xT_done, 4 * n + c + 1)
                    for k in range(2):
                        kt = 4 * c + k
                        o = ps[:, kt * SEQ:(kt + 1) * SEQ]
                        last = nc.scalar.activation(o, o, ACT.Identity, bias=mod[:, 0, kt:kt + 1],
                                                    scale=mod[:, 1, kt:kt + 1])
                    last.then_inc(mod_act, 1)

                def halve(c):
                    act.wait_ge(mod_act, 4 * n + c + 1)
                    act.wait_ge(mod_dve, 4 * n + c + 1)
                    nc.scalar.activation(xT_hi[:, 4 * c:4 * c + 4, :],
                                         bank(2 * c, 2).rearrange("p (k s) -> p k s", k=4), ACT.Copy).then_inc(xh_done, 1)
                act.wait_ge(acc_free, ACC_CREDIT + 4 * SUMMED_AT[n])
                modulate(0)
                modulate(1)
                halve(0)
                modulate(2)
                halve(1)
                modulate(3)
                halve(2)
                halve(3)

            def copy_qT(u, heads=4):
                act.wait_ge(qT_done, u + 1)
                nc.scalar.activation(qT[:, 0:heads, :], bank(4, 2).rearrange("p (h s) -> p h s", h=4)[:, 0:heads, :],
                                     ACT.Copy).then_inc(qT_copied, 1)

            def exps(u, scale, c=False):
                act.wait_ge(top_done, u + 1)
                if c:
                    nc.scalar.activation(sinke[:, :, :], sinkd[:, :, :], ACT.Exp)
                for t in range(TT):
                    for h in range(4):
                        src = ps[:, 4 * 512 + 256 * h:4 * 512 + 256 * h + 256] if t else \
                            ps[:, 6 * 512 + 128 * h:6 * 512 + 128 * h + 128]
                        last = nc.scalar.activation(probs[:, h, 128 * t:128 + 256 * t], src, ACT.Exp,
                                                    bias=negtop[:, t, h:h + 1], scale=scale,
                                                    accum_out=den[:, t, h:h + 1])
                last.then_inc(probs_done, 1)

            def copy_pT(h, done, n=384):
                act.wait_ge(pT_done, done)
                nc.scalar.activation(probs[:, h, 0:n], ps[:, (7 - h % 2) * 512:(7 - h % 2) * 512 + n],
                                     ACT.Copy).then_inc(pT_act, 1)

            def sub_norm(u):
                act.wait_ge(o_done, u + 1)
                act.wait_ge(y_done, u)
                for t in range(TT):
                    for h in range(2):
                        last = nc.scalar.activation(y[:, t, 256 * h:256 * h + 256],
                                                    ps[:, (4 + t) * 512 + 256 * h:(4 + t) * 512 + 256 * h + 256],
                                                    ACT.Square, accum_out=ssq[:, 4 + 2 * t + h:5 + 2 * t + h])
                last.then_inc(sub_sq, 1)
                act.wait_ge(sub_ms, u - 1)
                nc.scalar.activation(rstd[:, 4:8], ssq[:, 4:8], ACT.Sqrt).then_inc(sub_root, 1)

            def y_hi(u, at, n):
                act.wait_ge(yT_done, u + 1)
                nc.scalar.activation(hT_hi[:, ds(at, n), :],
                                     ps[:, 6 * 512:6 * 512 + n * SEQ].rearrange("p (k s) -> p k s", k=n),
                                     ACT.Copy).then_inc(yTh_done, 1)

            act.wait_ge(s_cond, 16)
            nc.scalar.activation(cond[:, :], cond[:, :], ACT.Silu).then_inc(s_silu_c, 1)
            act.wait_ge(s_const, 16 * CONSTS)
            act.wait_ge(s_setup, 4)
            nc.scalar.activation(lam[:, 2:4], lam[:, 0:2], ACT.Exp).then_inc(s_setup, 1)
            norm(0, s_x, 16)
            norm_out(0)

            def ab_stage(n, u, kind):
                B = kind == "B"
                if n == 5:
                    exps(u, 128 ** -0.5)
                if n == 8:
                    copy_pT(0, heads_before(u, kind) + 1)
                if n == 10 and not B:
                    copy_pT(2, heads_before(u, kind) + 3)
                if n == 12 and B:
                    sub_norm(u)
                if n == 15:
                    y_hi(u, 4 * u, 4)

            def ab(i, prev):
                for n in range(24):
                    hi(AB_IN, i, n)
                    if prev:
                        ab_stage(n, i - 1, prev)
                    if n == 16:
                        copy_qT(i)
            ab(0, None)
            repeat(act, 1, 3, lambda i: ab(i, "A"))
            ab(3, "B")
            for n in range(5, 16):
                ab_stage(n, 3, "B")

            def rest(ph, first=0):
                for p in range(first, ph.blocks * ph.pairs):
                    hi(ph, 0, p)
                repeat(act, 1, ph.n, lambda i: [hi(ph, i, p) for p in range(ph.blocks * ph.pairs)])

            def ffn(layer, n_norm):
                h0 = 22 * layer

                def silu_step(ph, h0, j, b):
                    blk = ph.block0 + j
                    act.wait_ge(pair_used, USED_CREDIT + 2 * ph.quad0 + 8 * (j + 1))
                    act.wait_ge(evacuated, blk + 1)
                    nc.scalar.activation(silu[:, b, :, :],
                                         bank(2 * b, 2).rearrange("p (t n) -> p t n", t=TT)[:, :, 0:HB],
                                         ACT.Silu).then_inc(silu_done, 1)

                def hidden_hi(h0, j, b):
                    act.wait_ge(hidT_done, HT_CREDIT + h0 + j + 1)
                    nc.scalar.activation(hT_hi[:, ds(2 * j, 2), :], bank(4 + b).rearrange("p (k s) -> p k s", k=2),
                                         ACT.Copy).then_inc(hTh_done, 1)
                for s, (fin, fout) in enumerate(FFN[layer]):
                    def body(i, first=False):
                        for b in range(2):
                            for p in range(8):
                                hi(fin, i, 8 * b + p)
                                if first and b == 0:
                                    continue
                                if p == 3:
                                    silu_step(fin, h0, 2 * i + b - 1, 1 - b)
                                if p == 5:
                                    hidden_hi(h0, 2 * i + b - 1, 1 - b)
                    body(0, True)
                    repeat(act, 1, fin.n, body)
                    for p in range(4):
                        hi(fout, 0, p)
                    silu_step(fin, h0, 2 * fin.n - 1, 1)
                    hidden_hi(h0, 2 * fin.n - 1, 1)
                    rest(fout, 4)
                    h0 += 2 * fin.n

            rest(AB_OUT)
            norm(1, evacuated, EVAC_CREDIT + AB_OUT.block0 + 4)
            norm_out(1)
            ffn(0, 1)
            norm(2, evacuated, EVAC_CREDIT + C_KV.block0)
            norm_out(2)
            for p in range(8):
                hi(C_KV, 0, p)

            def c_unit(u):
                exps(u, 64 ** -0.5, c=True)
                copy_pT(0, heads_before(u, "C") + 1)
                copy_pT(2, heads_before(u, "C") + 3)
                y_hi(u, 2 * (u - 4), 2)

            def c_attention(c):
                copy_qT(4 + c)
                for half in range(2):
                    c_unit(4 + 2 * c + half)

            def cq(i, first=False):
                for b in range(2):
                    for p in range(8):
                        hi(C_Q, i, 8 * b + p)
                        if p == 3 and not (first and b == 0):
                            c_attention(2 * i + b - 1)
            cq(0, True)
            repeat(act, 1, C_Q.n, cq)
            c_attention(3)
            rest(C_OUT)
            norm(3, evacuated, EVAC_CREDIT + C_OUT.block0 + 4)
            norm_out(3)
            ffn(1, 3)
            norm(4, evacuated, EVAC_CREDIT + chain[-1].block0 + 4)

        @block.vector
        def _(dve):
            tt = nc.vector.tensor_tensor
            stt = nc.vector.scalar_tensor_tensor

            def lo(ph, i, p):
                dve.wait_ge(hi_ready, ph.pair(i, p) + 1)
                tt(w_lo[:, p % PAIRS, :, :], raw[:, (p // 2) % RAW, 2 * (p % 2):2 * (p % 2) + 2, :],
                   w_hi[:, p % PAIRS, :, :].bitcast(F32), ALU.subtract).then_inc(lo_ready, 1)

            def ada(ph, i, a):
                q = ph.ada_quad(i, a)
                j = i * ph.ada + a // 4
                dve.wait_ge(ada_landed[a % ADA_RAW], 16 * ph.ada_fills(i, a))
                if a % 4 == 0:
                    dve.wait_ge(acc_free, ph.ada0 + j + 1)
                dst = acc[:, ds(ph.ada0 % ACC + j, 1), :].rearrange("p a n -> p (a n)")
                for k in range(4):
                    kt = 4 * (a % 4) + k
                    src = ada_raw[:, a % ADA_RAW, k, :]
                    dve.wait_ge(ada_step, ADA_CREDIT + 4 * q + k)
                    if kt == 0:
                        nc.vector.tensor_scalar(dst, src, cond[:, kt:kt + 1], None, ALU.mult).then_inc(ada_step, 1)
                    else:
                        stt(out=dst, in0=src, scalar=cond[:, kt:kt + 1], in1=dst, op0=ALU.mult,
                            op1=ALU.add).then_inc(ada_step, 1)

            def split(ph, i, p):
                lo(ph, i, p)
                if p % 2:
                    for a in ph.ada_after(p // 2):
                        ada(ph, i, a)

            def columns(n, layer, vec, dst, extra):
                dve.wait_ge(mods_summed, n + 1)
                stt(out=mod[:, dst, :], in0=ps[:, 7 * 512:7 * 512 + KT], scalar=extra, in1=ada_bias[:, layer, vec, :],
                    op0=ALU.add, op1=ALU.add).then_inc(acc_free, 4)

            def gate_row(n, landed):
                dve.wait_ge(mods_summed, n + 1)
                dve.wait_ge(gate_landed, 16 * landed)
                tt(gate[:, :], bank(4, 4), gate[:, :], ALU.add).then_inc(acc_free, 4)

            def norm(n):
                dve.wait_ge(ssq_done, n + 1)
                nc.vector.tensor_scalar(ssq[:, 2:4], ssq[:, 0:2], 1.0 / D, RMS_EPS, ALU.mult, ALU.add).then_inc(ms_done, 1)
                dve.wait_ge(root_done, n + 1)
                nc.vector.reciprocal(rstd[:, 0:2], rstd[:, 2:4])
                dve.drain()
                for t in range(TT):
                    ins = nc.vector.tensor_scalar(xn[:, t, :], x[:, t, :], rstd[:, t:t + 1], None, ALU.mult)
                    if n < 4:
                        ins.then_inc(xn_done, 1)

            def norm_out(n):
                def modulate(c):
                    dve.wait_ge(xT_done, 4 * n + c + 1)
                    for k in range(2, 4):
                        kt = 4 * c + k
                        o = ps[:, kt * SEQ:(kt + 1) * SEQ]
                        last = nc.vector.tensor_scalar(o, o, mod[:, 1, kt:kt + 1], mod[:, 0, kt:kt + 1], ALU.mult, ALU.add)
                    last.then_inc(mod_dve, 1)

                def rest(c):
                    dve.wait_ge(xh_done, 4 * n + c + 1)
                    tt(xT_lo[:, 4 * c:4 * c + 4, :], bank(2 * c, 2).rearrange("p (k s) -> p k s", k=4),
                       xT_hi[:, 4 * c:4 * c + 4, :].bitcast(F32), ALU.subtract).then_inc(xl_done, 1)
                dve.wait_ge(acc_free, ACC_CREDIT + 4 * SUMMED_AT[n])
                modulate(0)
                modulate(1)
                rest(0)
                modulate(2)
                rest(1)
                modulate(3)
                rest(2)
                rest(3)

            def rope(dst, src, table, t, heads, d):
                half = d // 2
                cos = table[:, t, 0, :].unsqueeze(1)
                sin = table[:, t, 1, :].unsqueeze(1)
                tmp = rope_t[:, 0:heads * d].rearrange("p (h d) -> p h d", h=heads)
                tt(tmp[:, :, 0:half], src[:, :, half:d], sin[:, :, 0:half].broadcast_to([P, heads, half]), ALU.mult)
                tt(tmp[:, :, half:d], src[:, :, 0:half], sin[:, :, half:d].broadcast_to([P, heads, half]), ALU.mult)
                tt(dst, src, cos.broadcast_to([P, heads, d]), ALU.mult)
                dve.drain()
                last = tt(dst, dst, tmp, ALU.add)
                return last

            def ab_rope(i, b):
                dve.wait_ge(pair_used, AB_IN.used(i, b))
                if b == 1:
                    dve.wait_ge(qT_done, i + 1)
                for t in range(TT):
                    last = rope(nat[:, t, :].rearrange("p (h d) -> p h d", h=4),
                                bank(2 * b + t).rearrange("p (h d) -> p h d", h=4), rope_ab, t, 4, 128)
                    dve.drain()
                nc.vector.engine_nop().then_inc(evacuated, 1)
                nc.vector.engine_nop().then_inc(roped, 1)

            def ab_v(i):
                dve.wait_ge(pair_used, AB_IN.used(i, 2))
                nc.vector.tensor_copy(v_ab, bank(0, 2).rearrange("p (t n) -> p t n", t=TT)).then_inc(evacuated, 1)

            def copy_kT(i):
                dve.wait_ge(kT_done, i + 1)
                nc.vector.tensor_copy(kT, bank(6, 2).rearrange("p (h s) -> p h s", h=4)).then_inc(kT_copied, 1)

            def tops(u, scale, c_at=None):
                dve.wait_ge(scores_done, u + 1)
                nc.vector.tensor_reduce(top[:, 0, :], bank(6).rearrange("p (h s) -> p h s", h=4), AX_X, ALU.max)
                nc.vector.tensor_reduce(top[:, 1, :], bank(4, 2).rearrange("p (h s) -> p h s", h=4), AX_X, ALU.max)
                dve.drain()
                if c_at is None:
                    nc.vector.tensor_scalar(negtop[:, :, :], top[:, :, :], -scale, None, ALU.mult).then_inc(top_done, 1)
                    return
                sink = sinks[:, ds(c_at, 4)]
                for t in range(TT):
                    stt(out=top[:, t, :], in0=top[:, t, :], scalar=scale, in1=sink, op0=ALU.mult, op1=ALU.max)
                dve.drain()
                for t in range(TT):
                    tt(sinkd[:, t, :], sink, top[:, t, :], ALU.subtract)
                nc.vector.tensor_scalar(negtop[:, :, :], top[:, :, :], -1.0, None, ALU.mult).then_inc(top_done, 1)

            def recip(u, c=False):
                dve.wait_ge(probs_done, u + 1)
                if c:
                    tt(den[:, :, :], den[:, :, :], sinke[:, :, :], ALU.add)
                    dve.drain()
                nc.vector.reciprocal(rden[:, :, :], den[:, :, :])
                dve.drain()

            def combine(u):
                recip(u)
                for h in range(2):
                    nc.vector.tensor_scalar(rden[:, :, 2 * h + 1], rden[:, :, 2 * h + 1], lam[:, 0:1], None, ALU.mult)
                    for t in range(TT):
                        w = probs[:, 2 * h, 128 * t:128 + 256 * t]
                        nc.vector.tensor_scalar(w, w, rden[:, t, 2 * h:2 * h + 1], None, ALU.mult)
                dve.drain()
                for h in range(2):
                    for t in range(TT):
                        w = probs[:, 2 * h, 128 * t:128 + 256 * t]
                        last = stt(out=w, in0=probs[:, 2 * h + 1, 128 * t:128 + 256 * t],
                                   scalar=rden[:, t, 2 * h + 1:2 * h + 2], in1=w, op0=ALU.mult, op1=ALU.add)
                last.then_inc(w_done, 1)

            def copy_pT(h, done, where):
                dve.wait_ge(pT_done, done)
                nc.vector.tensor_copy(probs[:, where, 0:384], ps[:, (7 - h % 2) * 512:(7 - h % 2) * 512 + 384]).then_inc(pT_dve, 1)

            def y_out(u, kind):
                dve.wait_ge(o_done, u + 1)
                n, d = (4, 64) if kind == "C" else (4, 128)
                if kind == "B":
                    dve.wait_ge(sub_sq, u - 1)
                    nc.vector.tensor_scalar(ssq[:, 4:8], ssq[:, 4:8], 1.0 / 256, SUBLN_EPS, ALU.mult, ALU.add).then_inc(sub_ms, 1)
                    dve.wait_ge(sub_root, u - 1)
                    nc.vector.reciprocal(rstd[:, 4:8], rstd[:, 4:8])
                    dve.drain()
                    nc.vector.tensor_scalar(rstd[:, 4:8], rstd[:, 4:8], 1.0 - LAMBDA_INIT, None, ALU.mult)
                    dve.drain()
                    for t in range(TT):
                        for h in range(2):
                            last = stt(out=y[:, t, 256 * h:256 * h + 256],
                                       in0=ps[:, (4 + t) * 512 + 256 * h:(4 + t) * 512 + 256 * h + 256],
                                       scalar=rstd[:, 4 + 2 * t + h:5 + 2 * t + h], in1=subln[:, :],
                                       op0=ALU.mult, op1=ALU.mult)
                else:
                    dst = y if kind == "A" else y_c
                    for t in range(TT):
                        last = tt(dst[:, t, 0:n * d].rearrange("p (h d) -> p h d", h=n),
                                  bank(4 + t)[:, 0:n * d].rearrange("p (h d) -> p h d", h=n),
                                  rden[:, t, :].unsqueeze(2).broadcast_to([P, n, d]), ALU.mult)
                last.then_inc(y_done, 1)

            def y_lo(u, at, n):
                dve.wait_ge(yTh_done, u + 1)
                tt(hT_lo[:, ds(at, n), :], ps[:, 6 * 512:6 * 512 + n * SEQ].rearrange("p (k s) -> p k s", k=n),
                   hT_hi[:, ds(at, n), :].bitcast(F32), ALU.subtract).then_inc(yTl_done, 1)

            y_c = q_c

            dve.wait_ge(s_const, 16 * CONSTS)
            nc.vector.tensor_copy(ident_b[:, :], ident[:, :])
            nc.vector.tensor_copy(mask_own[:, :], work[:, 0:128])
            nc.vector.tensor_copy(mask_prev[:, :], work[:, 128:256])
            lv = work[:, 256:768].rearrange("p (a b n) -> p a b n", a=2, b=2)
            prod = work[:, 768:1024].rearrange("p (a n) -> p a n", a=2)
            tt(prod, lv[:, :, 0, :], lv[:, :, 1, :], ALU.mult)
            dve.drain()
            nc.vector.tensor_reduce(lam[:, 0:2], prod, AX_X, ALU.add).then_inc(s_setup, 2)
            dve.wait_ge(s_setup, 5)
            tt(lam[:, 0:1], lam[:, 3:4], lam[:, 2:3], ALU.subtract)
            dve.drain()
            nc.vector.tensor_scalar(lam[:, 0:1], lam[:, 0:1], -LAMBDA_INIT, None, ALU.add).then_inc(s_setup, 1)
            dve.wait_ge(s_silu_c, 1)
            repeat(dve, 0, MOD0.n, lambda i: [ada(MOD0, i, a) for a in range(4)])
            columns(0, 0, 0, 0, 0.0)
            columns(1, 0, 1, 1, 1.0)
            norm(0)
            norm_out(0)

            def ab_stage(n, u, kind):
                B = kind == "B"
                if n == 3:
                    ab_v(u)
                if n == 5:
                    tops(u, 128 ** -0.5)
                if n == 6:
                    if B:
                        combine(u)
                    else:
                        recip(u)
                if n == 8:
                    copy_pT(1, heads_before(u, kind) + 2, 2 if B else 1)
                if n == 10 and not B:
                    copy_pT(3, heads_before(u, kind) + 4, 3)
                if n == 12:
                    y_out(u, kind)
                if n == 15:
                    y_lo(u, 4 * u, 4)

            def ab(i, prev):
                for n in range(24):
                    split(AB_IN, i, n)
                    if prev:
                        ab_stage(n, i - 1, prev)
                    if n == 11:
                        ab_rope(i, 0)
                    if n == 19:
                        ab_rope(i, 1)
                    if n == 23:
                        copy_kT(i)
            ab(0, None)
            repeat(dve, 1, 3, lambda i: ab(i, "A"))
            ab(3, "B")
            for n in range(3, 16):
                ab_stage(n, 3, "B")
            gate_row(G1[0], 1)
            columns(SH2[0], 0, 3, 0, 0.0)

            def project(ph, bias=False, first=0):
                def update(j, b, nth):
                    dve.wait_ge(pair_used, USED_CREDIT + 2 * ph.quad0 + ph.pairs * (j + 1))
                    src = bank(2 * b, 2).rearrange("p (t n) -> p t n", t=TT)
                    g = gate[:, ds(j * NT, NT)].unsqueeze(1).broadcast_to([P, TT, NT])
                    if bias:
                        dve.wait_ge(bo_landed[b], 16 * nth)
                        tt(upd, src, bias_o[:, b:b + 1, :].broadcast_to([P, TT, NT]), ALU.add)
                        dve.drain()
                        src = upd
                    tt(upd, src, g, ALU.mult)
                    dve.drain()
                    xs = x[:, :, ds(j * NT, NT)]
                    tt(xs, xs, upd, ALU.add).then_inc(evacuated, 1)

                def body(i, peeled=False):
                    for b in range(2):
                        for p in range(ph.pairs):
                            if peeled and b * ph.pairs + p < first:
                                continue
                            split(ph, i, b * ph.pairs + p)
                            if p == 3 and not (peeled and b == 0):
                                update(2 * i + b - 1, 1 - b, i + b)
                body(0, True)
                repeat(dve, 1, ph.n, body)
                update(2 * ph.n - 1, 1, ph.n)

            def ffn(layer):
                h0 = 22 * layer

                def gated(ph, h0, j, b):
                    dve.wait_ge(silu_done, h0 + j + 1)
                    dve.wait_ge(hidT_done, h0 + j + 1)
                    tt(hid[:, b, :, :], bank(2 * b, 2).rearrange("p (t n) -> p t n", t=TT)[:, :, HB:2 * HB],
                       silu[:, b, :, :], ALU.mult).then_inc(evacuated, 1)

                def hidden_lo(h0, j, b):
                    dve.wait_ge(hTh_done, h0 + j + 1)
                    tt(hT_lo[:, ds(2 * j, 2), :], bank(4 + b).rearrange("p (k s) -> p k s", k=2),
                       hT_hi[:, ds(2 * j, 2), :].bitcast(F32), ALU.subtract).then_inc(hTl_done, 1)
                for s, (fin, fout) in enumerate(FFN[layer]):
                    def body(i, first=False):
                        for b in range(2):
                            for p in range(8):
                                split(fin, i, 8 * b + p)
                                if first and b == 0:
                                    continue
                                if p == 3:
                                    gated(fin, h0, 2 * i + b - 1, 1 - b)
                                if p == 5:
                                    hidden_lo(h0, 2 * i + b - 1, 1 - b)
                    body(0, True)
                    repeat(dve, 1, fin.n, body)
                    for p in range(4):
                        split(fout, 0, p)
                    gated(fin, h0, 2 * fin.n - 1, 1)
                    hidden_lo(h0, 2 * fin.n - 1, 1)
                    h0 += 2 * fin.n
                    if s == 0:
                        gate_row(G2[layer], 2 + 2 * layer)
                    if layer == 0 and s == 1:
                        columns(SC1[1], 1, 1, 1, 1.0)
                    project(fout, first=4)
                    if layer == 0 and s == 0:
                        columns(SH1[1], 1, 0, 0, 0.0)

            project(AB_OUT)
            columns(SC2[0], 0, 4, 1, 1.0)
            norm(1)
            norm_out(1)
            ffn(0)
            norm(2)
            norm_out(2)
            for p in range(8):
                split(C_KV, 0, p)

            def biased(ph, i, b, slot, c):
                dve.wait_ge(pair_used, ph.used(i, b))
                dve.wait_ge(bias_landed, 16 * (c + 1))
                tt(q_c, bank(2 * slot, 2).rearrange("p (t n) -> p t n", t=TT),
                   bias_c.unsqueeze(1).broadcast_to([P, TT, NT]), ALU.add).then_inc(evacuated, 1)
                dve.drain()

            def c_keys():
                nc.vector.memset(work[:, 0:2048], 0.0)
                biased(C_KV, 0, 0, 0, 0)
                for t in range(TT):
                    rope(k_c[:, t, :, 0, 0:64], q_c[:, t, 0:256].rearrange("p (h d) -> p h d", h=4), rope_c, t, 4, 64)
                    dve.drain()
                    nc.vector.tensor_copy(k_c[:, t, :, 1, 64:128], k_c[:, t, :, 0, 0:64])
                nc.vector.tensor_copy(v_c, q_c[:, :, 256:512]).then_inc(roped, 1)
                dve.wait_ge(kT_done, 5)
                nc.vector.tensor_copy(kT_c[:, 0:4, :], bank(4, 2).rearrange("p (g s) -> p g s", g=4))
                nc.vector.tensor_copy(kT_c[:, 4:8, :], bank(6, 2).rearrange("p (g s) -> p g s", g=4)).then_inc(kT_copied, 1)

            def c_attention(ph, i, b, c):
                biased(ph, i, b, 1 - b, c + 1)
                for t in range(TT):
                    last = rope(nat[:, t, :].rearrange("p (h d) -> p h d", h=8),
                                q_c[:, t, :].rearrange("p (h d) -> p h d", h=8), rope_c, t, 8, 64)
                    if t == 0:
                        dve.drain()
                last.then_inc(roped, 1)
                for half in range(2):
                    u = 4 + 2 * c + half
                    tops(u, 64 ** -0.5, c_at=8 * c + 4 * half)
                    recip(u, c=True)
                    copy_pT(1, heads_before(u, "C") + 2, 1)
                    copy_pT(3, heads_before(u, "C") + 4, 3)
                    y_out(u, "C")
                    y_lo(u, 2 * (u - 4), 2)

            def cq(i, first=False):
                for b in range(2):
                    for p in range(8):
                        split(C_Q, i, 8 * b + p)
                        if p == 3 and first and b == 0:
                            c_keys()
                            columns(SH2[1], 1, 3, 0, 0.0)
                        elif p == 3 and b == 0:
                            c_attention(C_Q, i - 1, 1, 2 * i - 1)
                        elif p == 3:
                            c_attention(C_Q, i, 0, 2 * i)
            cq(0, True)
            repeat(dve, 1, C_Q.n, cq)
            c_attention(C_Q, C_Q.n - 1, 1, 3)
            gate_row(G1[1], 3)
            project(C_OUT, bias=True)
            columns(SC2[1], 1, 4, 1, 1.0)
            norm(3)
            norm_out(3)
            ffn(1)
            norm(4)
            dve.drain()
            dve.wait_ge(gate_landed, 16 * 5)
            for t in range(TT):
                tt(xn[:, t, :], xn[:, t, :], gate[:, :], ALU.mult).then_inc(xn_done, 1)

        @block.tensor
        def _(pe):
            mm = nc.tensor.matmul

            def tr(out, in_):
                return nc.tensor.transpose(out, in_, ident[:, :])

            def pair(ph, i, b, p, slot, hi, lo):
                q = b * ph.pairs + p
                pe.wait_ge(lo_ready, LO_CREDIT + ph.pair(i, q) + 1)
                for k in range(2):
                    kt = 2 * p + k
                    for t in range(TT):
                        out = bank(2 * slot + t)
                        tok = slice(t * P, (t + 1) * P)
                        mm(out, hi[:, kt, tok], w_hi[:, q % PAIRS, k, :], start=(kt == 0), stop=False)
                        mm(out, hi[:, kt, tok], w_lo[:, q % PAIRS, k, :], start=False, stop=False)
                        last = mm(out, lo[:, kt, tok], w_hi[:, q % PAIRS, k, :], start=False,
                                  stop=(kt == 2 * ph.pairs - 1))
                last.then_inc(pair_used, 1)

            def sum_columns(n, slot0, last_ada):
                pe.wait_ge(ada_step, ADA_CREDIT + 16 * last_ada)
                pe.wait_ge(acc_free, ACC_CREDIT + 4 * n)
                for c in range(KT):
                    last = mm(ps[:, 7 * 512 + c:7 * 512 + c + 1], acc[:, slot0 + c // 4, (c % 4) * P:(c % 4 + 1) * P],
                              ones[:, 0:1], start=True, stop=True)
                last.then_inc(mods_summed, 1)

            def sum_row(n, slot0, last_ada):
                pe.wait_ge(ada_step, ADA_CREDIT + 16 * last_ada)
                pe.wait_ge(acc_free, ACC_CREDIT + 4 * n)
                for c in range(NB):
                    last = mm(bank(4 + c), ones[:, :], acc[:, slot0 + c, :], start=True, stop=True)
                last.then_inc(mods_summed, 1)

            def norm(n):
                pe.wait_ge(xn_done, 2 * n + 2)
                for c in range(4):
                    for k in range(4):
                        kt = 4 * c + k
                        for t in range(TT):
                            last = tr(ps[:, kt * SEQ + t * P:kt * SEQ + (t + 1) * P], xn[:, t, kt * P:(kt + 1) * P])
                    last.then_inc(xT_done, 1)

            def q_transposes(i, c=False):
                pe.wait_ge(roped, 9 + i - 4 if c else 2 * i + 1)
                for h in range(4):
                    for t in range(TT):
                        last = tr(ps[:, 4 * 512 + h * SEQ + t * P:4 * 512 + h * SEQ + (t + 1) * P],
                                  nat[:, t, h * P:(h + 1) * P])
                last.then_inc(qT_done, 1)

            def k_transposes(i):
                pe.wait_ge(roped, 2 * i + 2)
                for h in range(4):
                    for t in range(TT):
                        last = tr(ps[:, 6 * 512 + h * SEQ + t * P:6 * 512 + h * SEQ + (t + 1) * P],
                                  nat[:, t, h * P:(h + 1) * P])
                last.then_inc(kT_done, 1)

            def scores(q, k, prev_mask):
                for h in range(4):
                    s0 = ps[:, 6 * 512 + h * P:6 * 512 + (h + 1) * P]
                    s1 = 4 * 512 + h * SEQ
                    mm(s0, ident_b[:, :], mask_own[:, :], start=True, stop=False)
                    mm(s0, q(h)[:, 0:P], k(h)[:, 0:P], start=False, stop=True)
                    if prev_mask:
                        mm(ps[:, s1:s1 + P], ident_b[:, :], mask_prev[:, :], start=True, stop=False)
                    mm(ps[:, s1:s1 + P], q(h)[:, P:SEQ], k(h)[:, 0:P], start=not prev_mask, stop=True)
                    mm(ps[:, s1 + P:s1 + SEQ], ident_b[:, :], mask_own[:, :], start=True, stop=False)
                    last = mm(ps[:, s1 + P:s1 + SEQ], q(h)[:, P:SEQ], k(h)[:, P:SEQ], start=False, stop=True)
                last.then_inc(scores_done, 1)

            def p_transposes(h, where):
                at = (7 - h % 2) * 512
                for b in range(3):
                    last = tr(ps[:, at + b * P:at + (b + 1) * P], probs[:, where, b * P:(b + 1) * P])
                last.then_inc(pT_done, 1)

            def outputs(heads, where, v, d):
                for h in range(heads):
                    o = slice(h * d, (h + 1) * d)
                    pT = probs[:, where(h), :]
                    mm(bank(4)[:, o], pT[:, 0:P], v(h, 0), start=True, stop=True)
                for h in range(heads):
                    o = slice(h * d, (h + 1) * d)
                    pT = probs[:, where(h), :]
                    mm(bank(5)[:, o], pT[:, P:2 * P], v(h, 0), start=True, stop=False)
                    last = mm(bank(5)[:, o], pT[:, 2 * P:3 * P], v(h, 1), start=False, stop=True)
                last.then_inc(o_done, 1)

            def y_transposes(u, src, n):
                pe.wait_ge(y_done, u + 1)
                for k in range(n):
                    for t in range(TT):
                        last = tr(ps[:, 6 * 512 + k * SEQ + t * P:6 * 512 + k * SEQ + (t + 1) * P],
                                  src[:, t, k * P:(k + 1) * P])
                last.then_inc(yT_done, 1)

            pe.wait_ge(s_const, 16 * CONSTS)
            pe.wait_ge(s_setup, 6)
            sum_columns(0, 0, 4)
            sum_columns(1, 4, 8)
            pe.wait_ge(acc_free, ACC_CREDIT + 8)
            norm(0)

            def ab_stage(n, u, kind):
                B = kind == "B"
                if n == 0:
                    pe.wait_ge(qT_copied, u + 1)
                    pe.wait_ge(kT_copied, u + 1)
                    scores(lambda h: qT[:, h, :], lambda h: kT[:, h, :], False)
                if n == 4:
                    if B:
                        pe.wait_ge(w_done, u - 1)
                    else:
                        pe.wait_ge(probs_done, u + 1)
                    p_transposes(0, 0)
                    p_transposes(1, 2 if B else 1)
                if n == 6 and not B:
                    pe.wait_ge(pT_act, 2 * u + 1)
                    p_transposes(2, 2)
                    pe.wait_ge(pT_dve, 2 * u + 1)
                    p_transposes(3, 3)
                if n == 8:
                    done = u + 3 if B else 2 * u + 2
                    pe.wait_ge(pT_act, done)
                    pe.wait_ge(pT_dve, done)
                    pe.wait_ge(evacuated, EVAC_CREDIT + 3 * u + 3)
                    if B:
                        outputs(2, lambda h: 2 * h, lambda h, t: v_ab[:, t, 256 * h:256 * h + 256], 256)
                    else:
                        outputs(4, lambda h: h, lambda h, t: v_ab[:, t, 128 * h:128 * h + 128], 128)
                if n == 11:
                    y_transposes(u, y, 4)

            def ab(i, prev):
                for b in range(3):
                    pe.wait_ge(evacuated, AB_IN.block(i, b) + (2 if b == 0 else 1) if b or prev else 2)
                    for p in range(8):
                        n = 8 * b + p
                        if prev is None and b == 0 and p % 2 == 0:
                            pe.wait_ge(xl_done, p // 2 + 1)
                        if prev is None and b == 1 and p == 0:
                            pe.wait_ge(xl_done, 4)
                        pair(AB_IN, i, b, p, b % 2, xT_hi, xT_lo)
                        if prev:
                            ab_stage(n, i - 1, prev)
                        if n == 12:
                            q_transposes(i)
                        if n == 20:
                            if prev:
                                pe.wait_ge(yTl_done, i)
                            k_transposes(i)
            ab(0, None)
            repeat(pe, 1, 3, lambda i: ab(i, "A"))
            ab(3, "B")
            for n in range(12):
                ab_stage(n, 3, "B")
            pe.wait_ge(yTl_done, 4)
            sum_row(G1[0], 0, 12)
            sum_columns(SH2[0], 4, 16)

            def blocks(ph, hi, lo, slot=0, before=None, after=None, x_at=None):
                def body(i, first=False):
                    for b in range(ph.blocks):
                        sl = (slot + b) % 2
                        if before:
                            before(i, b)
                        pe.wait_ge(evacuated, ph.block(i, b) + 1)
                        for p in range(ph.pairs):
                            if first and b == 0 and x_at is not None and p % 2 == 0:
                                pe.wait_ge(xl_done, 4 * x_at + p // 2 + 1)
                            pair(ph, i, b, p, sl, hi, lo)
                            if after and p == 2 and not (first and b == 0):
                                after(ph.blocks * i + b - 1, 1 - b)
                body(0, True)
                repeat(pe, 1, ph.n, body)

            def ffn(layer, n_norm):
                h0 = 22 * layer
                for s, (fin, fout) in enumerate(FFN[layer]):
                    def hid_transposes(j, b):
                        pe.wait_ge(evacuated, EVAC_CREDIT + fin.block0 + j + 1)
                        pe.wait_ge(hTl_done, h0 + j + 1)
                        for k in range(2):
                            for t in range(TT):
                                last = tr(ps[:, (4 + b) * 512 + k * SEQ + t * P:(4 + b) * 512 + k * SEQ + (t + 1) * P],
                                          hid[:, b, t, k * P:(k + 1) * P])
                        last.then_inc(hidT_done, 1)
                    blocks(fin, xT_hi, xT_lo, after=hid_transposes, x_at=n_norm if s == 0 else None)
                    hid_transposes(2 * fin.n - 1, 1)
                    h0 += 2 * fin.n
                    pe.wait_ge(hTl_done, HT_CREDIT + h0)
                    if s == 0:
                        sum_row(G2[layer], 4, 24 if layer == 0 else 48)
                    if layer == 0 and s == 1:
                        sum_columns(SC1[1], 4, 32)
                    blocks(fout, hT_hi, hT_lo)
                    if layer == 0 and s == 0:
                        sum_columns(SH1[1], 0, 28)

            blocks(AB_OUT, hT_hi, hT_lo)
            sum_columns(SC2[0], 0, 20)
            pe.wait_ge(acc_free, ACC_CREDIT + 20)
            norm(1)
            ffn(0, 1)
            norm(2)
            blocks(C_KV, xT_hi, xT_lo, x_at=2)

            def c_keys():
                pe.wait_ge(roped, 9)
                for g in range(8):
                    for t in range(TT):
                        last = tr(ps[:, 4 * 512 + g * SEQ + t * P:4 * 512 + g * SEQ + (t + 1) * P],
                                  k_c[:, t, g // 2, g % 2, :])
                last.then_inc(kT_done, 1)
                pe.wait_ge(kT_copied, 5)
                sum_columns(SH2[1], 4, 40)

            def c_attention(c):
                q_transposes(4 + c + 1, c=True)
                pe.wait_ge(qT_copied, 5 + c)
                kk = [kT_c[:, ds(2 * c + e, 1), :].rearrange("p a s -> p (a s)") for e in range(2)]
                for half in range(2):
                    u = 4 + 2 * c + half
                    pe.wait_ge(yTl_done, u)
                    scores(lambda h: qT[:, 2 * half + h // 2, :], lambda h: kk[h % 2], True)
                    pe.wait_ge(probs_done, u + 1)
                    p_transposes(0, 0)
                    p_transposes(1, 1)
                    pe.wait_ge(pT_act, 2 * u - 1)
                    p_transposes(2, 2)
                    pe.wait_ge(pT_dve, 2 * u - 1)
                    p_transposes(3, 3)
                    pe.wait_ge(pT_act, 2 * u)
                    pe.wait_ge(pT_dve, 2 * u)
                    outputs(4, lambda h: h, lambda h, t: v_c[:, t, ds(64 * c, 64)], 64)
                    y_transposes(u, q_c, 2)
                pe.wait_ge(yTl_done, 6 + 2 * c)

            def c_before(i, b):
                if isinstance(i, int) and i == 0 and b == 0:
                    c_keys()
                else:
                    c_attention(2 * i + b - 1)
            blocks(C_Q, xT_hi, xT_lo, slot=1, before=c_before)
            c_attention(3)
            sum_row(G1[1], 0, 36)
            blocks(C_OUT, hT_hi, hT_lo)
            sum_columns(SC2[1], 0, 44)
            pe.wait_ge(acc_free, ACC_CREDIT + 44)
            norm(3)
            ffn(1, 3)
    return nc


def quads(w, blocks):
    k = w.shape[0]
    t = w.reshape(k // 512, 4, P, blocks, NT)
    return np.ascontiguousarray(t.transpose(3, 0, 2, 1, 4)).reshape(-1, P, 4 * NT)


def rope_table(dim):
    freq = np.float32(10000.0) ** (-np.arange(0, dim, 2, dtype=np.float32) / np.float32(dim))
    angle = np.arange(SEQ, dtype=np.float32)[:, None] * freq[None, :]
    cos, sin = np.cos(angle), np.sin(angle)
    t = np.stack([np.concatenate([cos, cos], -1), np.concatenate([-sin, sin], -1)], 1).astype(np.float32)
    return np.ascontiguousarray(t.reshape(TT, P, 2, dim).transpose(1, 0, 2, 3))


def layouts(i):
    ada_w, ada_b = i["ada_w"], i["ada_b"]
    ab = quads(i["ab_w_in"][0], 12).reshape(12, 4, P, 4 * NT)
    order = [6 * (u // 2) + u % 2 + 2 * b for u in range(4) for b in range(3)]
    swa = quads(i["swa_w_in"][0], 5).reshape(5, 4, P, 4 * NT)
    ffn_in, ffn_out = [], []
    for w_in, w_out in zip(i["ffn_w_in"], i["ffn_w_out"]):
        pairs = w_in.reshape(D, 2, HID // HB, HB).transpose(0, 2, 1, 3).reshape(D, 2 * HID)
        ffn_in.append(quads(pairs, HID // HB))
        at = 0
        for kts in SPLITS:
            ffn_out.append(quads(w_out[at * P:(at + kts) * P], NB))
            at += kts
    key, query = np.arange(P)[None, :], np.arange(P)[:, None]
    masks = np.concatenate([np.where(key <= query, 0.0, MASKED), np.where(key > query, 0.0, MASKED)], 1)
    gates = ada_b.reshape(2, 6, D)[:, [2, 5]].reshape(4, D)
    return {
        "x": i["x"].reshape(SEQ, D),
        "c": i["c"].reshape(KT, P).T,
        "ada": np.concatenate([quads(w, ADA_COLS // NT) for w in ada_w]),
        "ada_bias": ada_b.reshape(2, 6, KT, P).transpose(3, 0, 1, 2),
        "gate_bias": gates,
        "ab_in": ab[order].reshape(-1, P, 4 * NT),
        "ab_out": quads(i["ab_w_out"][0], NB),
        "swa_in": swa[[4, 0, 1, 2, 3]].reshape(-1, P, 4 * NT),
        "swa_out": quads(i["swa_w_out"][0], NB),
        "swa_b_in": i["swa_b_in"].reshape(5, NT)[[4, 0, 1, 2, 3]],
        "swa_b_out": i["swa_b_out"].reshape(NB, NT),
        "ffn_in": np.concatenate(ffn_in),
        "ffn_out": np.concatenate(ffn_out),
        "subln": i["diff_subln"].reshape(256),
        "sinks": i["swa_sinks"].reshape(32),
        "lam": i["diff_lambda"].reshape(512),
        "final_norm": i["final_norm"],
        "ident": np.eye(P, dtype=np.float32),
        "masks": masks.astype(np.float32),
        "rope_ab": rope_table(128),
        "rope_c": rope_table(64),
    }


def kernel(**inputs):
    import concourse.bacc as bacc
    from concourse.bass_utils import run_bass_kernel_spmd as run

    arrays = {k: np.ascontiguousarray(v) for k, v in layouts({k: np.asarray(v) for k, v in inputs.items()}).items()}
    nc = bacc.Bacc("TRN2", target_bir_lowering=False, num_devices=1)
    T = {k: nc.dram_tensor(f"in_{k}", v.shape, F32, kind="ExternalInput").ap() for k, v in arrays.items()}
    T["out"] = nc.dram_tensor("out", (SEQ, D), F32, kind="ExternalOutput").ap()
    for name in ("x", "out"):
        T[name] = T[name].rearrange("(t p) d -> p t d", p=P)
    kernel_program(nc, T)
    r = run(nc, [{f"in_{k}": v for k, v in arrays.items()}], core_ids=[0])
    return r.results[0]["out"].reshape(1, SEQ, D)
```

```python
from contextlib import ExitStack

import numpy as np

import concourse.bass as bass
from concourse import mybir

ALU = mybir.AluOpType
ACT = mybir.ActivationFunctionType
F32 = mybir.dt.float32
F32R = mybir.dt.float32r
BF16 = mybir.dt.bfloat16
AX_X = mybir.AxisListType.X
ds = bass.ds

P = 128
D = 2048
SEQ = 256
TT = SEQ // P
NT = 512
KT = D // P
NB = D // NT
HID = 5632
HB = 256
ADA_COLS = 6 * D
RAW = 4
PAIRS = 4
ADA_RAW = 2
ACC = 8
MOD0_BLOCKS = 8
SPLITS = (16, 16, 12)
LAMBDA_INIT = 0.2
RMS_EPS = 1e-6
SUBLN_EPS = 1e-5
MASKED = -1e30

LO_CREDIT = 2 * RAW
USED_CREDIT = PAIRS
ADA_CREDIT = 4 * ADA_RAW
ACC_CREDIT = ACC
EVAC_CREDIT = 2
HT_CREDIT = 2


class Phase:

    def __init__(self, prev, n, blocks, pairs, ada, src=None, src0=0):
        self.n, self.blocks, self.pairs, self.ada = n, blocks, pairs, ada
        self.quads = blocks * pairs // 2
        self.src, self.src0 = src, src0
        self.quad0 = prev.quad0 + prev.n * prev.quads if prev else 0
        self.block0 = prev.block0 + prev.n * prev.blocks if prev else 0
        self.ada0 = prev.ada0 + prev.n * prev.ada if prev else 0
        self.fills = [len(range(s, self.quads, RAW)) for s in range(RAW)]
        self.fills0 = [a + prev.n * b for a, b in zip(prev.fills0, prev.fills)] if prev else [0] * RAW

    def quad(self, i, t):
        return self.quad0 + i * self.quads + t

    def pair(self, i, p):
        return 2 * self.quad0 + i * (2 * self.quads) + p

    def block(self, i, b):
        return self.block0 + i * self.blocks + b

    def ada_quad(self, i, a):
        return 4 * self.ada0 + i * (4 * self.ada) + a

    def raw_fills(self, i, t):
        s = t % RAW
        return self.fills0[s] + i * self.fills[s] + t // RAW + 1

    def raw_distance(self, t):
        if t >= RAW or self.quads % RAW == 0:
            return RAW
        last = max(u for u in range(self.quads) if u % RAW == t % RAW)
        return self.quads - last + t

    def used(self, i, b):
        return USED_CREDIT + self.pair(i, (b + 1) * self.pairs)

    def ada_fills(self, i, a):
        return 2 * self.ada0 - MOD0_BLOCKS + i * (2 * self.ada) + a // ADA_RAW + 1

    def ada_after(self, t):
        n = 4 * self.ada
        return range(n * t // self.quads, n * (t + 1) // self.quads)


SH1, SC1, G1, SH2, SC2, G2 = ((v, v + 6) for v in range(6))
SUMMED_AT = (2, 5, 8, 11)

AB_PE = {0: "scores", 4: "pT01", 6: "pT23", 8: "out", 11: "yT"}
AB_ACT = {5: "exps", 8: "copy0", 10: "copy2", 12: "norm", 15: "hi"}
AB_DVE = {3: "v", 5: "tops", 6: "recip", 8: "copy1", 10: "copy3", 12: "y", 15: "lo"}
TAIL_PE = {0: "scores", 3: "pT01", 4: "out", 5: "yT"}
TAIL_ACT = {4: "exps", 6: "copy0", 8: "norm", 9: "hi"}
TAIL_DVE = {3: "v", 4: "tops", 5: "recip", 6: "copy1", 8: "y", 9: "lo"}
C_PE = {0: "scores", 3: "pT01", 4: "pT23", 5: "out", 6: "yT"}
C_ACT = {4: "exps", 7: "copy0", 8: "copy2", 10: "hi"}
C_DVE = {4: "tops", 6: "recip", 7: "copy1", 8: "copy3", 9: "y", 10: "lo"}
C_UNITS = 8
C_LAST = 8 * 5 + 11


def c_base(w):
    return 8 * (w // 2) + 12 + 4 * (w % 2)


def heads_before(u, kind):
    return {"A": 4 * u, "B": 2 * u + 4, "C": 4 * u - 4}[kind]


def kernel_program(nc, T):
    chain = []

    def phase(*a, **k):
        chain.append(Phase(chain[-1] if chain else None, *a, **k))
        return chain[-1]

    MOD0 = phase(MOD0_BLOCKS // 2, 0, 0, 2)
    MOD0.fills = [1] * RAW
    AB_IN = phase(4, 3, 8, 2, src="ab_in")
    AB_OUT = phase(2, 2, 8, 2, src="ab_out")
    FFN = []
    C_KV = C_Q = C_OUT0 = C_OUT1 = None
    for layer in range(2):
        at_in, at_out, runs = layer * (HID // HB) * 4, layer * (HID // P), []
        for s, kts in enumerate(SPLITS):
            in_ada = int(layer == 0 or s == 0)
            out_ada = (2, 2, 1)[s] if layer == 0 else 0
            runs.append((phase(kts // 4, 2, 8, in_ada, src="ffn_in", src0=at_in),
                         phase(2, 2, kts // 2, out_ada, src="ffn_out", src0=at_out)))
            at_in += kts // 2 * 4
            at_out += kts
        FFN.append(runs)
        if layer == 0:
            C_KV = phase(1, 1, 8, 1, src="swa_in")
            C_Q = phase(4, 1, 8, 0, src="swa_in", src0=4)
            C_OUT0 = phase(1, 1, 8, 0, src="swa_out")
            C_OUT1 = phase(1, 3, 8, 2, src="swa_out", src0=4)
    assert chain[-1].ada0 == 48

    with ExitStack() as ctx:
        def sb(name, shape, dt=F32):
            return ctx.enter_context(nc.sbuf_tensor(name, shape, dt))

        def sem(name):
            return ctx.enter_context(nc.semaphore(name))

        x = sb("x", [P, TT, D])
        xT_hi = sb("xT_hi", [P, KT, SEQ], F32R)
        xT_lo = sb("xT_lo", [P, KT, SEQ], F32R)
        hT_hi = sb("hT_hi", [P, KT, SEQ], F32R)
        hT_lo = sb("hT_lo", [P, KT, SEQ], F32R)
        raw = sb("raw", [P, RAW, 4, NT])
        w_hi = sb("w_hi", [P, PAIRS, 2, NT], F32R)
        w_lo = sb("w_lo", [P, PAIRS, 2, NT], F32R)
        ada_raw = sb("ada_raw", [P, ADA_RAW, 4, NT])
        acc = sb("acc", [P, ACC, NT])
        work = sb("work", [P, 4096])
        gate = sb("gate", [P, D])
        ident = sb("ident", [P, P])
        ones = sb("ones", [P, P])
        ident_b = sb("ident_b", [P, P], BF16)
        mask_own = sb("mask_own", [P, P], BF16)
        mask_prev = sb("mask_prev", [P, P], BF16)
        rope_ab = sb("rope_ab", [P, TT, 2, 128])
        rope_c = sb("rope_c", [P, TT, 2, 64])
        subln = sb("subln", [P, 256])
        sinks = sb("sinks", [P, 32])
        cond = sb("cond", [P, KT])
        ada_bias = sb("ada_bias", [P, 2, 6, KT])
        mod = sb("mod", [P, 2, 6, KT])
        ssq = sb("ssq", [P, 8])
        rstd = sb("rstd", [P, 8])
        top = sb("top", [P, TT, 4])
        negtop = sb("negtop", [P, TT, 4])
        den = sb("den", [P, TT, 4])
        rden = sb("rden", [P, TT, 4])
        sinkd = sb("sinkd", [P, TT, 4])
        sinke = sb("sinke", [P, TT, 4])
        lam = sb("lam", [P, 4])

        ps = ctx.enter_context(nc.psum_tensor("ps", [P, 8 * 512], F32))

        def bank(b, n=1):
            return ps[:, b * 512:(b + n) * 512]

        nat = work[:, 0:1024].rearrange("p (t n) -> p t n", t=TT)
        qT = work[:, 1024:2048].rearrange("p (h s) -> p h s", h=4)
        y = work[:, 1024:2048].rearrange("p (t n) -> p t n", t=TT)
        kT = work[:, 2048:3072].rearrange("p (h s) -> p h s", h=4)
        v_ab = work[:, 3072:4096].rearrange("p (t n) -> p t n", t=TT)
        q_c = v_ab
        y_c = q_c
        k_c = work[:, 0:2048].rearrange("p (t g e n) -> p t g e n", t=TT, g=4, e=2)
        bias_c = work[:, 2048:2560]
        probs = gate[:, 0:1536].rearrange("p (h n) -> p h n", h=4)
        probs_c = [probs, ada_raw[:, 1, 1:4, :].rearrange("p a n -> p (a n)").rearrange("p (h n) -> p h n", h=4)]
        rope_t = gate[:, 1536:2048]
        kT_c = acc[:, 4:8, :].rearrange("p a n -> p (a n)").rearrange("p (g s) -> p g s", g=8)
        v_c = ada_raw[:, 1, 0, :].rearrange("p (t n) -> p t n", t=TT)
        silu = work[:, 0:1024].rearrange("p (b t n) -> p b t n", b=2, t=TT)
        hid = work[:, 1024:2048].rearrange("p (b t n) -> p b t n", b=2, t=TT)
        upd = work[:, 2048:3072].rearrange("p (t n) -> p t n", t=TT)
        bias_o = work[:, 3072:4096].rearrange("p (b n) -> p b n", b=2)
        xn = work[:, :].rearrange("p (t n) -> p t n", t=TT)

        s_x = sem("x_landed")
        s_const = sem("constants_landed")
        s_cond = sem("cond_landed")
        raw_landed = [sem(f"raw_landed{s}") for s in range(RAW)]
        ada_landed = [sem(f"ada_landed{s}") for s in range(ADA_RAW)]
        final_landed = sem("final_norm_landed")
        gate_spread = sem("gate_spread")
        gate_copied = sem("gate_copied")
        bias_landed = sem("c_bias_landed")
        bo_landed = [sem(f"c_out_bias_landed{s}") for s in range(2)]
        hi_ready = sem("hi_ready")
        lo_ready = sem("lo_ready")
        pair_used = sem("pair_used")
        evacuated = sem("evacuated")
        s_setup = sem("setup_done")
        s_silu_c = sem("silu_c_done")
        ada_step = sem("ada_step")
        mods_summed = sem("mods_summed")
        acc_free = sem("acc_free")
        ssq_done = sem("ssq_done")
        ms_done = sem("mean_square_done")
        root_done = sem("root_done")
        xn_done = sem("xn_done")
        xT_done = sem("xT_done")
        mod_act = sem("modulated_act")
        mod_dve = sem("modulated_dve")
        xh_done = sem("xT_hi_done")
        xl_done = sem("xT_lo_done")
        silu_done = sem("silu_done")
        hidT_done = sem("hidT_done")
        hTh_done = sem("hT_hi_done")
        hTl_done = sem("hT_lo_done")
        roped = sem("roped")
        qT_done = sem("qT_done")
        qT_copied = sem("qT_copied")
        kT_done = sem("kT_done")
        kT_copied = sem("kT_copied")
        scores_done = sem("scores_done")
        top_done = sem("top_done")
        probs_done = sem("probs_done")
        w_done = sem("w_done")
        pT_done = sem("pT_done")
        pT_act = sem("pT_copied_act")
        pT_dve = sem("pT_copied_dve")
        o_done = sem("o_done")
        sub_sq = sem("subln_square_done")
        sub_ms = sem("subln_mean_done")
        sub_root = sem("subln_root_done")
        y_done = sem("y_done")
        yT_done = sem("yT_done")
        yTh_done = sem("yT_hi_done")
        yTl_done = sem("yT_lo_done")
        out_landed = sem("out_landed")

        CONSTS = 8
        block = ctx.enter_context(nc.Block())

        def repeat(eng, lo, hi, body):
            if hi - lo == 1:
                body(lo)
            elif hi > lo:
                with eng.Fori(lo, hi) as i:
                    body(i)

        @block.sync
        def _(sp):
            sp.dma_start(cond[:, :], T["c"]).then_inc(s_cond, 16)

            def ada(ph, i, a):
                q = ph.ada_quad(i, a)
                sp.wait_ge(ada_step, 4 * q + 4)
                sp.dma_start(ada_raw[:, a % ADA_RAW, :, :].rearrange("p a n -> p (a n)"),
                             T["ada"][q]).then_inc(ada_landed[a % ADA_RAW], 16)

            def mod0(i):
                for a in range(8):
                    q = MOD0.ada_quad(i, a)
                    s, ring = (a // 4 * 2 + a % 2, raw) if a % 4 >= 2 else (a % 2, ada_raw)
                    back = 8 if ring is raw else 4
                    if not isinstance(i, int) or q >= back:
                        sp.wait_ge(ada_step, ADA_CREDIT + 4 * (q - back + 1))
                    sp.dma_start(ring[:, s, :, :].rearrange("p a n -> p (a n)"), T["ada"][q])\
                        .then_inc((raw_landed if ring is raw else ada_landed)[s], 16)

            def body(ph, i):
                for t in range(ph.quads):
                    sp.wait_ge(lo_ready, LO_CREDIT + 2 * (ph.quad(i, t) - ph.raw_distance(t) + 1))
                    if ph is AB_IN and t < RAW and isinstance(i, int):
                        sp.wait_ge(ada_step, ADA_CREDIT + 4 * (MOD0.ada_quad(MOD0.n - 1, (2, 3, 6, 7)[t]) + 1))
                    sp.dma_start(raw[:, t % RAW, :, :].rearrange("p a n -> p (a n)"),
                                 T[ph.src][ph.src0 + i * ph.quads + t]).then_inc(raw_landed[t % RAW], 16)
                    for a in ph.ada_after(t):
                        if ph is C_OUT1 and a == 0:
                            sp.wait_ge(o_done, 12)
                        ada(ph, i, a)

            repeat(sp, 0, 1, mod0)
            sp.dma_start(x[:, :, :], T["x"]).then_inc(s_x, 16)
            repeat(sp, 1, MOD0.n, mod0)
            for n, ph in enumerate(chain[1:]):
                if chain[n].quads % RAW:
                    sp.wait_ge(lo_ready, LO_CREDIT + 2 * ph.quad0)
                repeat(sp, 0, 1, lambda i: body(ph, i))
                repeat(sp, 1, ph.n, lambda i: body(ph, i))

            sp.wait_ge(xn_done, 10)
            sp.dma_start(T["out"], xn).then_inc(out_landed, 16)
            sp.wait_ge(out_landed, 16)

        @block.gpsimd
        def _(pool):
            pool.sem_inc(lo_ready, LO_CREDIT)
            pool.sem_inc(pair_used, USED_CREDIT)
            pool.sem_inc(ada_step, ADA_CREDIT)
            pool.sem_inc(acc_free, ACC_CREDIT)
            pool.sem_inc(evacuated, EVAC_CREDIT)
            pool.sem_inc(hidT_done, HT_CREDIT)
            pool.sem_inc(hTl_done, HT_CREDIT)
            pool.memset(ones[:, :], 1.0).then_inc(s_setup, 2)
            for dst, name in ((ident[:, :], "ident"), (rope_ab[:, :, :, :], "rope_ab"), (rope_c[:, :, :, :], "rope_c"),
                              (ada_bias[:, :, :, :], "ada_bias"), (work[:, 0:256], "masks")):
                pool.dma_start(dst, T[name]).then_inc(s_const, 16)
            for dst, name in ((subln[:, :], "subln"), (sinks[:, :], "sinks"), (work[:, 256:768], "lam")):
                pool.dma_start(dst, T[name].partition_broadcast(P)).then_inc(s_const, 16)

            for c in range(5):
                if c == 0:
                    pool.wait_ge(xT_done, 12)
                else:
                    pool.wait_ge(evacuated, EVAC_CREDIT + C_KV.block0 + c)
                pool.dma_start(bias_c, T["swa_b_in"][c].partition_broadcast(P)).then_inc(bias_landed, 16)
            pool.wait_ge(yT_done, 12)
            for n in range(NB):
                pool.wait_ge(evacuated, C_OUT0.block0 + n + 1)
                pool.dma_start(bias_o[:, n % 2, :],
                               T["swa_b_out"][n].partition_broadcast(P)).then_inc(bo_landed[n % 2], 16)
            pool.wait_ge(evacuated, EVAC_CREDIT + chain[-1].block0 + 4)
            pool.dma_start(gate[:, :], T["final_norm"].partition_broadcast(P)).then_inc(final_landed, 16)

        @block.scalar
        def _(act):
            def hi(ph, i, p):
                t = p // 2
                if p % 2 == 0:
                    act.wait_ge(raw_landed[t % RAW], 16 * ph.raw_fills(i, t))
                act.wait_ge(pair_used, ph.pair(i, p) + 1)
                nc.scalar.activation(w_hi[:, p % PAIRS, :, :], raw[:, t % RAW, 2 * (p % 2):2 * (p % 2) + 2, :],
                                     ACT.Copy).then_inc(hi_ready, 1)

            def norm(n, x_ready, ready):
                act.wait_ge(x_ready, ready)
                for t in range(TT):
                    last = nc.scalar.activation(xn[:, t, :], x[:, t, :], ACT.Square, accum_out=ssq[:, t:t + 1])
                last.then_inc(ssq_done, 1)
                act.wait_ge(ms_done, n + 1)
                nc.scalar.activation(rstd[:, 2:4], ssq[:, 2:4], ACT.Sqrt).then_inc(root_done, 1)

            def norm_out(n):
                shift, scale = mod[:, n // 2, 3 * (n % 2), :], mod[:, n // 2, 3 * (n % 2) + 1, :]

                def modulate(c):
                    act.wait_ge(xT_done, 4 * n + c + 1)
                    for k in range(2):
                        kt = 4 * c + k
                        o = ps[:, kt * SEQ:(kt + 1) * SEQ]
                        last = nc.scalar.activation(o, o, ACT.Identity, bias=shift[:, kt:kt + 1],
                                                    scale=scale[:, kt:kt + 1])
                    last.then_inc(mod_act, 1)

                def halve(c):
                    act.wait_ge(mod_act, 4 * n + c + 1)
                    act.wait_ge(mod_dve, 4 * n + c + 1)
                    nc.scalar.activation(xT_hi[:, 4 * c:4 * c + 4, :],
                                         bank(2 * c, 2).rearrange("p (k s) -> p k s", k=4), ACT.Copy).then_inc(xh_done, 1)
                act.wait_ge(acc_free, ACC_CREDIT + 4 * SUMMED_AT[n])
                modulate(0)
                modulate(1)
                halve(0)
                modulate(2)
                halve(1)
                modulate(3)
                halve(2)
                halve(3)

            def copy_qT(u):
                act.wait_ge(qT_done, u + 1)
                nc.scalar.activation(qT, bank(4, 2).rearrange("p (h s) -> p h s", h=4), ACT.Copy).then_inc(qT_copied, 1)

            def exps(u, scale, pr, c=False):
                act.wait_ge(top_done, u + 1)
                if c:
                    nc.scalar.activation(sinke[:, :, :], sinkd[:, :, :], ACT.Exp)
                for t in range(TT):
                    for h in range(4):
                        src = ps[:, 4 * 512 + 256 * h:4 * 512 + 256 * h + 256] if t else \
                            ps[:, 6 * 512 + 128 * h:6 * 512 + 128 * h + 128]
                        last = nc.scalar.activation(pr[:, h, 128 * t:128 + 256 * t], src, ACT.Exp,
                                                    bias=negtop[:, t, h:h + 1], scale=scale,
                                                    accum_out=den[:, t, h:h + 1])
                last.then_inc(probs_done, 1)

            def copy_pT(dst, done):
                act.wait_ge(pT_done, done)
                nc.scalar.activation(dst, bank(7)[:, 0:384], ACT.Copy).then_inc(pT_act, 1)

            def sub_norm(u):
                act.wait_ge(o_done, u + 1)
                act.wait_ge(y_done, u)
                for t in range(TT):
                    for h in range(2):
                        last = nc.scalar.activation(y[:, t, 256 * h:256 * h + 256],
                                                    ps[:, (4 + t) * 512 + 256 * h:(4 + t) * 512 + 256 * h + 256],
                                                    ACT.Square, accum_out=ssq[:, 4 + 2 * t + h:5 + 2 * t + h])
                last.then_inc(sub_sq, 1)
                act.wait_ge(sub_ms, u - 1)
                nc.scalar.activation(rstd[:, 4:8], ssq[:, 4:8], ACT.Sqrt).then_inc(sub_root, 1)

            def y_hi(u, at, n, b):
                act.wait_ge(yT_done, u + 1)
                nc.scalar.activation(hT_hi[:, ds(at, n), :], ps[:, b * 512:b * 512 + n * SEQ].rearrange("p (k s) -> p k s", k=n),
                                     ACT.Copy).then_inc(yTh_done, 1)

            act.wait_ge(s_cond, 16)
            nc.scalar.activation(cond[:, :], cond[:, :], ACT.Silu).then_inc(s_silu_c, 1)
            act.wait_ge(s_const, 16 * CONSTS)
            act.wait_ge(s_setup, 4)
            nc.scalar.activation(lam[:, 2:4], lam[:, 0:2], ACT.Exp).then_inc(s_setup, 1)
            norm(0, s_x, 16)
            norm_out(0)

            def ab_stage(stage, u, kind):
                if stage == "exps":
                    exps(u, 128 ** -0.5, probs)
                if stage == "copy0":
                    copy_pT(probs[:, 0, :], heads_before(u, kind) + 1)
                if stage == "copy2" and kind == "A":
                    copy_pT(probs[:, 2, :], heads_before(u, kind) + 3)
                if stage == "norm" and kind == "B":
                    sub_norm(u)
                if stage == "hi":
                    y_hi(u, 4 * u, 4, 6)

            def ab(i, prev):
                for n in range(24):
                    hi(AB_IN, i, n)
                    if prev:
                        ab_stage(AB_ACT.get(n), i - 1, prev)
                    if n == 16:
                        copy_qT(i)
            ab(0, None)
            repeat(act, 1, 3, lambda i: ab(i, "A"))
            ab(3, "B")
            for n in range(16):
                hi(AB_OUT, 0, n)
                ab_stage(TAIL_ACT.get(n), 3, "B")
            repeat(act, 1, AB_OUT.n, lambda i: [hi(AB_OUT, i, p) for p in range(16)])

            def rest(ph, first=0):
                for p in range(first, ph.blocks * ph.pairs):
                    hi(ph, 0, p)
                repeat(act, 1, ph.n, lambda i: [hi(ph, i, p) for p in range(ph.blocks * ph.pairs)])

            def ffn(layer, n_norm):
                h0 = 22 * layer

                def silu_step(ph, h0, j, b):
                    blk = ph.block0 + j
                    act.wait_ge(pair_used, USED_CREDIT + 2 * ph.quad0 + 8 * (j + 1))
                    act.wait_ge(evacuated, blk + 1)
                    nc.scalar.activation(silu[:, b, :, :],
                                         bank(2 * b, 2).rearrange("p (t n) -> p t n", t=TT)[:, :, 0:HB],
                                         ACT.Silu).then_inc(silu_done, 1)

                def hidden_hi(h0, j, b):
                    act.wait_ge(hidT_done, HT_CREDIT + h0 + j + 1)
                    nc.scalar.activation(hT_hi[:, ds(2 * j, 2), :], bank(4 + b).rearrange("p (k s) -> p k s", k=2),
                                         ACT.Copy).then_inc(hTh_done, 1)
                for s, (fin, fout) in enumerate(FFN[layer]):
                    def body(i, first=False):
                        for b in range(2):
                            for p in range(8):
                                hi(fin, i, 8 * b + p)
                                if first and b == 0:
                                    continue
                                if p == 3:
                                    silu_step(fin, h0, 2 * i + b - 1, 1 - b)
                                if p == 5:
                                    hidden_hi(h0, 2 * i + b - 1, 1 - b)
                    body(0, True)
                    repeat(act, 1, fin.n, body)
                    for p in range(4):
                        hi(fout, 0, p)
                    silu_step(fin, h0, 2 * fin.n - 1, 1)
                    hidden_hi(h0, 2 * fin.n - 1, 1)
                    rest(fout, 4)
                    h0 += 2 * fin.n

            norm(1, evacuated, EVAC_CREDIT + AB_OUT.block0 + 4)
            norm_out(1)
            ffn(0, 1)
            norm(2, evacuated, EVAC_CREDIT + C_KV.block0)
            norm_out(2)
            for p in range(8):
                hi(C_KV, 0, p)

            def c_stages(g):
                for w in range(C_UNITS):
                    u, stage = 4 + w, C_ACT.get(g - c_base(w))
                    pr = probs_c[w % 2]
                    if stage == "exps":
                        exps(u, 64 ** -0.5, pr, c=True)
                    if stage == "copy0":
                        copy_pT(pr[:, 0, :], heads_before(u, "C") + 1)
                    if stage == "copy2":
                        copy_pT(pr[:, 2, :], heads_before(u, "C") + 3)
                    if stage == "hi":
                        y_hi(u, 2 * w, 2, 7)
                for c in range(4):
                    for half, at in ((0, 6), (1, 10)):
                        if g == 8 * (c + 1) + at:
                            act.wait_ge(qT_done, 5 + 2 * c + half)
                            nc.scalar.activation(qT[:, 2 * half:2 * half + 2, :],
                                                 bank(2).rearrange("p (h s) -> p h s", h=2), ACT.Copy).then_inc(qT_copied, 1)
            for c in range(4):
                for p in range(8):
                    hi(C_Q, c, p)
                    c_stages(8 * c + p)
            for p in range(8):
                hi(C_OUT0, 0, p)
                c_stages(32 + p)
            for g in range(40, C_LAST):
                c_stages(g)
            for p in range(24):
                hi(C_OUT1, 0, p)
            norm(3, evacuated, EVAC_CREDIT + C_OUT0.block0 + 4)
            norm_out(3)
            ffn(1, 3)
            norm(4, evacuated, EVAC_CREDIT + chain[-1].block0 + 4)

        @block.vector
        def _(dve):
            tt = nc.vector.tensor_tensor
            stt = nc.vector.scalar_tensor_tensor

            def lo(ph, i, p):
                dve.wait_ge(hi_ready, ph.pair(i, p) + 1)
                tt(w_lo[:, p % PAIRS, :, :], raw[:, (p // 2) % RAW, 2 * (p % 2):2 * (p % 2) + 2, :],
                   w_hi[:, p % PAIRS, :, :].bitcast(F32), ALU.subtract).then_inc(lo_ready, 1)

            def ada(ph, i, a):
                q = ph.ada_quad(i, a)
                j = i * ph.ada + a // 4
                if ph is MOD0:
                    ring, s = (raw, a // 4 * 2 + a % 2) if a % 4 >= 2 else (ada_raw, a % 2)
                    landed = raw_landed[s] if ring is raw else ada_landed[s]
                    dve.wait_ge(landed, 16 * (i + 1) if ring is raw else 16 * (2 * i + a // 4 + 1))
                else:
                    ring, s = ada_raw, a % ADA_RAW
                    dve.wait_ge(ada_landed[s], 16 * ph.ada_fills(i, a))
                if a % 4 == 0:
                    dve.wait_ge(acc_free, ph.ada0 + j + 1)
                slot = (ph.ada0 + j) % ACC if isinstance(j, int) else ph.ada0 % ACC + j
                dst = acc[:, ds(slot, 1), :].rearrange("p a n -> p (a n)")
                for k in range(4):
                    kt = 4 * (a % 4) + k
                    src = ring[:, s, k, :]
                    dve.wait_ge(ada_step, ADA_CREDIT + 4 * q + k)
                    if kt == 0:
                        nc.vector.tensor_scalar(dst, src, cond[:, kt:kt + 1], None, ALU.mult).then_inc(ada_step, 1)
                    else:
                        stt(out=dst, in0=src, scalar=cond[:, kt:kt + 1], in1=dst, op0=ALU.mult,
                            op1=ALU.add).then_inc(ada_step, 1)

            def split(ph, i, p):
                lo(ph, i, p)
                if p % 2:
                    for a in ph.ada_after(p // 2):
                        ada(ph, i, a)

            def columns(n):
                layer, vec = n // 6, n % 6
                dve.wait_ge(mods_summed, n + 1)
                stt(out=mod[:, layer, vec, :], in0=ps[:, 7 * 512:7 * 512 + KT], scalar=float(vec % 3 == 1),
                    in1=ada_bias[:, layer, vec, :], op0=ALU.add, op1=ALU.add).then_inc(acc_free, 4)

            def gate_row(n):
                dve.wait_ge(gate_spread, n + 1)
                nc.vector.tensor_copy(gate[:, :], bank(4, 4)).then_inc(gate_copied, 1)
                dve.drain()

            def norm(n):
                dve.wait_ge(ssq_done, n + 1)
                nc.vector.tensor_scalar(ssq[:, 2:4], ssq[:, 0:2], 1.0 / D, RMS_EPS, ALU.mult, ALU.add).then_inc(ms_done, 1)
                dve.wait_ge(root_done, n + 1)
                nc.vector.reciprocal(rstd[:, 0:2], rstd[:, 2:4])
                dve.drain()
                for t in range(TT):
                    ins = nc.vector.tensor_scalar(xn[:, t, :], x[:, t, :], rstd[:, t:t + 1], None, ALU.mult)
                    if n < 4:
                        ins.then_inc(xn_done, 1)

            def norm_out(n):
                shift, scale = mod[:, n // 2, 3 * (n % 2), :], mod[:, n // 2, 3 * (n % 2) + 1, :]

                def modulate(c):
                    dve.wait_ge(xT_done, 4 * n + c + 1)
                    for k in range(2, 4):
                        kt = 4 * c + k
                        o = ps[:, kt * SEQ:(kt + 1) * SEQ]
                        last = nc.vector.tensor_scalar(o, o, scale[:, kt:kt + 1], shift[:, kt:kt + 1], ALU.mult, ALU.add)
                    last.then_inc(mod_dve, 1)

                def rest(c):
                    dve.wait_ge(xh_done, 4 * n + c + 1)
                    tt(xT_lo[:, 4 * c:4 * c + 4, :], bank(2 * c, 2).rearrange("p (k s) -> p k s", k=4),
                       xT_hi[:, 4 * c:4 * c + 4, :].bitcast(F32), ALU.subtract).then_inc(xl_done, 1)
                dve.wait_ge(acc_free, ACC_CREDIT + 4 * SUMMED_AT[n])
                modulate(0)
                modulate(1)
                rest(0)
                modulate(2)
                rest(1)
                modulate(3)
                rest(2)
                rest(3)

            def rope(dst, src, table, t, heads, d):
                half = d // 2
                cos = table[:, t, 0, :].unsqueeze(1)
                sin = table[:, t, 1, :].unsqueeze(1)
                tmp = rope_t[:, 0:heads * d].rearrange("p (h d) -> p h d", h=heads)
                tt(tmp[:, :, 0:half], src[:, :, half:d], sin[:, :, 0:half].broadcast_to([P, heads, half]), ALU.mult)
                tt(tmp[:, :, half:d], src[:, :, 0:half], sin[:, :, half:d].broadcast_to([P, heads, half]), ALU.mult)
                tt(dst, src, cos.broadcast_to([P, heads, d]), ALU.mult)
                dve.drain()
                last = tt(dst, dst, tmp, ALU.add)
                return last

            def ab_rope(i, b):
                dve.wait_ge(pair_used, AB_IN.used(i, b))
                if b == 1:
                    dve.wait_ge(qT_done, i + 1)
                for t in range(TT):
                    last = rope(nat[:, t, :].rearrange("p (h d) -> p h d", h=4),
                                bank(2 * b + t).rearrange("p (h d) -> p h d", h=4), rope_ab, t, 4, 128)
                    dve.drain()
                nc.vector.engine_nop().then_inc(evacuated, 1)
                nc.vector.engine_nop().then_inc(roped, 1)

            def ab_v(i):
                dve.wait_ge(pair_used, AB_IN.used(i, 2))
                nc.vector.tensor_copy(v_ab, bank(0, 2).rearrange("p (t n) -> p t n", t=TT)).then_inc(evacuated, 1)

            def copy_kT(i):
                dve.wait_ge(kT_done, i + 1)
                nc.vector.tensor_copy(kT, bank(6, 2).rearrange("p (h s) -> p h s", h=4)).then_inc(kT_copied, 1)

            def tops(u, scale, c_at=None):
                dve.wait_ge(scores_done, u + 1)
                nc.vector.tensor_reduce(top[:, 0, :], bank(6).rearrange("p (h s) -> p h s", h=4), AX_X, ALU.max)
                nc.vector.tensor_reduce(top[:, 1, :], bank(4, 2).rearrange("p (h s) -> p h s", h=4), AX_X, ALU.max)
                dve.drain()
                if c_at is None:
                    nc.vector.tensor_scalar(negtop[:, :, :], top[:, :, :], -scale, None, ALU.mult).then_inc(top_done, 1)
                    return
                sink = sinks[:, ds(c_at, 4)]
                for t in range(TT):
                    stt(out=top[:, t, :], in0=top[:, t, :], scalar=scale, in1=sink, op0=ALU.mult, op1=ALU.max)
                dve.drain()
                for t in range(TT):
                    tt(sinkd[:, t, :], sink, top[:, t, :], ALU.subtract)
                nc.vector.tensor_scalar(negtop[:, :, :], top[:, :, :], -1.0, None, ALU.mult).then_inc(top_done, 1)

            def recip(u, c=False):
                dve.wait_ge(probs_done, u + 1)
                if c:
                    tt(den[:, :, :], den[:, :, :], sinke[:, :, :], ALU.add)
                    dve.drain()
                nc.vector.reciprocal(rden[:, :, :], den[:, :, :])
                dve.drain()

            def combine(u):
                recip(u)
                for h in range(2):
                    nc.vector.tensor_scalar(rden[:, :, 2 * h + 1], rden[:, :, 2 * h + 1], lam[:, 0:1], None, ALU.mult)
                    for t in range(TT):
                        w = probs[:, 2 * h, 128 * t:128 + 256 * t]
                        nc.vector.tensor_scalar(w, w, rden[:, t, 2 * h:2 * h + 1], None, ALU.mult)
                dve.drain()
                for h in range(2):
                    for t in range(TT):
                        w = probs[:, 2 * h, 128 * t:128 + 256 * t]
                        last = stt(out=w, in0=probs[:, 2 * h + 1, 128 * t:128 + 256 * t],
                                   scalar=rden[:, t, 2 * h + 1:2 * h + 2], in1=w, op0=ALU.mult, op1=ALU.add)
                last.then_inc(w_done, 1)

            def copy_pT(dst, done, b):
                dve.wait_ge(pT_done, done)
                nc.vector.tensor_copy(dst, bank(b)[:, 0:384]).then_inc(pT_dve, 1)

            def y_out(u, kind):
                dve.wait_ge(o_done, u + 1)
                n, d = (4, 64) if kind == "C" else (4, 128)
                if kind == "B":
                    dve.wait_ge(sub_sq, u - 1)
                    nc.vector.tensor_scalar(ssq[:, 4:8], ssq[:, 4:8], 1.0 / 256, SUBLN_EPS, ALU.mult, ALU.add).then_inc(sub_ms, 1)
                    dve.wait_ge(sub_root, u - 1)
                    nc.vector.reciprocal(rstd[:, 4:8], rstd[:, 4:8])
                    dve.drain()
                    nc.vector.tensor_scalar(rstd[:, 4:8], rstd[:, 4:8], 1.0 - LAMBDA_INIT, None, ALU.mult)
                    dve.drain()
                    for t in range(TT):
                        for h in range(2):
                            last = stt(out=y[:, t, 256 * h:256 * h + 256],
                                       in0=ps[:, (4 + t) * 512 + 256 * h:(4 + t) * 512 + 256 * h + 256],
                                       scalar=rstd[:, 4 + 2 * t + h:5 + 2 * t + h], in1=subln[:, :],
                                       op0=ALU.mult, op1=ALU.mult)
                else:
                    for t in range(TT):
                        src = bank(4 + t) if kind == "A" else bank(3)[:, 256 * t:256 * t + 256]
                        dst = y[:, t, :] if kind == "A" else y_c[:, t, 0:256]
                        last = tt(dst.rearrange("p (h d) -> p h d", h=n), src.rearrange("p (h d) -> p h d", h=n),
                                  rden[:, t, :].unsqueeze(2).broadcast_to([P, n, d]), ALU.mult)
                last.then_inc(y_done, 1)

            def y_lo(u, at, n, b):
                dve.wait_ge(yTh_done, u + 1)
                tt(hT_lo[:, ds(at, n), :], ps[:, b * 512:b * 512 + n * SEQ].rearrange("p (k s) -> p k s", k=n),
                   hT_hi[:, ds(at, n), :].bitcast(F32), ALU.subtract).then_inc(yTl_done, 1)

            dve.wait_ge(s_const, 16 * CONSTS)
            nc.vector.tensor_copy(ident_b[:, :], ident[:, :])
            nc.vector.tensor_copy(mask_own[:, :], work[:, 0:128])
            nc.vector.tensor_copy(mask_prev[:, :], work[:, 128:256])
            lv = work[:, 256:768].rearrange("p (a b n) -> p a b n", a=2, b=2)
            prod = work[:, 768:1024].rearrange("p (a n) -> p a n", a=2)
            tt(prod, lv[:, :, 0, :], lv[:, :, 1, :], ALU.mult)
            dve.drain()
            nc.vector.tensor_reduce(lam[:, 0:2], prod, AX_X, ALU.add).then_inc(s_setup, 2)
            dve.wait_ge(s_setup, 5)
            tt(lam[:, 0:1], lam[:, 3:4], lam[:, 2:3], ALU.subtract)
            dve.drain()
            nc.vector.tensor_scalar(lam[:, 0:1], lam[:, 0:1], -LAMBDA_INIT, None, ALU.add).then_inc(s_setup, 1)
            dve.wait_ge(s_silu_c, 1)
            repeat(dve, 0, MOD0.n, lambda i: [ada(MOD0, i, a) for a in range(8)])
            columns(SH1[0])
            columns(SC1[0])
            norm(0)
            norm_out(0)

            def ab_stage(stage, u, kind):
                B = kind == "B"
                if stage == "v":
                    ab_v(u)
                if stage == "tops":
                    tops(u, 128 ** -0.5)
                if stage == "recip":
                    if B:
                        combine(u)
                    else:
                        recip(u)
                if stage == "copy1":
                    copy_pT(probs[:, 2 if B else 1, :], heads_before(u, kind) + 2, 6)
                if stage == "copy3" and not B:
                    copy_pT(probs[:, 3, :], heads_before(u, kind) + 4, 6)
                if stage == "y":
                    y_out(u, kind)
                if stage == "lo":
                    y_lo(u, 4 * u, 4, 6)

            def ab(i, prev):
                for n in range(24):
                    split(AB_IN, i, n)
                    if prev:
                        ab_stage(AB_DVE.get(n), i - 1, prev)
                    if n == 11:
                        ab_rope(i, 0)
                    if n == 19:
                        ab_rope(i, 1)
                    if prev == "B" and n == 21:
                        columns(G1[0])
                    if n == 23:
                        copy_kT(i)

            def update(j, b, used, nth=None):
                dve.wait_ge(pair_used, used)
                src = bank(2 * b, 2).rearrange("p (t n) -> p t n", t=TT)
                if nth is not None:
                    dve.wait_ge(bo_landed[j % 2], 16 * nth)
                    tt(upd, src, bias_o[:, j % 2:j % 2 + 1, :].broadcast_to([P, TT, NT]), ALU.add)
                    dve.drain()
                    src = upd
                tt(upd, src, gate[:, ds(j * NT, NT)].unsqueeze(1).broadcast_to([P, TT, NT]), ALU.mult)
                dve.drain()
                xs = x[:, :, ds(j * NT, NT)]
                tt(xs, xs, upd, ALU.add).then_inc(evacuated, 1)

            def project(ph, gate_n=None, first=0, slot=0, tail=None):
                def used(j):
                    return USED_CREDIT + 2 * ph.quad0 + ph.pairs * (j + 1)

                def body(i, peeled=False):
                    for b in range(2):
                        for p in range(ph.pairs):
                            n = b * ph.pairs + p
                            if not (peeled and n < first):
                                split(ph, i, n)
                            if peeled and tail:
                                ab_stage(tail.get(n), 3, "B")
                            if p == 3 and not (peeled and b == 0):
                                if peeled and gate_n is not None:
                                    if tail:
                                        columns(SH2[0])
                                    gate_row(gate_n)
                                j = 2 * i + b - 1
                                update(j, (slot + 1 - b) % 2, used(j))
                body(0, True)
                repeat(dve, 1, ph.n, body)
                update(2 * ph.n - 1, (slot + 1) % 2, used(2 * ph.n - 1))

            ab(0, None)
            repeat(dve, 1, 3, lambda i: ab(i, "A"))
            ab(3, "B")
            project(AB_OUT, gate_n=0, slot=1, tail=TAIL_DVE)
            columns(SC2[0])

            def ffn(layer):
                h0 = 22 * layer

                def gated(ph, h0, j, b):
                    dve.wait_ge(silu_done, h0 + j + 1)
                    dve.wait_ge(hidT_done, h0 + j + 1)
                    tt(hid[:, b, :, :], bank(2 * b, 2).rearrange("p (t n) -> p t n", t=TT)[:, :, HB:2 * HB],
                       silu[:, b, :, :], ALU.mult).then_inc(evacuated, 1)

                def hidden_lo(h0, j, b):
                    dve.wait_ge(hTh_done, h0 + j + 1)
                    tt(hT_lo[:, ds(2 * j, 2), :], bank(4 + b).rearrange("p (k s) -> p k s", k=2),
                       hT_hi[:, ds(2 * j, 2), :].bitcast(F32), ALU.subtract).then_inc(hTl_done, 1)
                for s, (fin, fout) in enumerate(FFN[layer]):
                    def body(i, first=False):
                        for b in range(2):
                            for p in range(8):
                                split(fin, i, 8 * b + p)
                                if first and b == 0:
                                    continue
                                if p == 3:
                                    gated(fin, h0, 2 * i + b - 1, 1 - b)
                                if p == 5:
                                    hidden_lo(h0, 2 * i + b - 1, 1 - b)
                    body(0, True)
                    repeat(dve, 1, fin.n, body)
                    for p in range(4):
                        split(fout, 0, p)
                    gated(fin, h0, 2 * fin.n - 1, 1)
                    hidden_lo(h0, 2 * fin.n - 1, 1)
                    h0 += 2 * fin.n
                    if s == 0:
                        columns(G2[layer])
                    if layer == 0 and s == 1:
                        columns(SC1[1])
                    project(fout, gate_n=1 + 2 * layer if s == 0 else None, first=4)
                    if layer == 0:
                        columns((SH1, G1, SH2)[s][1])

            norm(1)
            norm_out(1)
            ffn(0)
            norm(2)
            norm_out(2)
            for p in range(8):
                split(C_KV, 0, p)

            def biased(ph, i, c):
                dve.wait_ge(pair_used, ph.used(i, 0))
                dve.wait_ge(bias_landed, 16 * (c + 1))
                tt(q_c, bank(0, 2).rearrange("p (t n) -> p t n", t=TT),
                   bias_c.unsqueeze(1).broadcast_to([P, TT, NT]), ALU.add).then_inc(evacuated, 1)
                dve.drain()

            def c_keys():
                nc.vector.memset(work[:, 0:2048], 0.0)
                biased(C_KV, 0, 0)
                for t in range(TT):
                    rope(k_c[:, t, :, 0, 0:64], q_c[:, t, 0:256].rearrange("p (h d) -> p h d", h=4), rope_c, t, 4, 64)
                    dve.drain()
                    nc.vector.tensor_copy(k_c[:, t, :, 1, 64:128], k_c[:, t, :, 0, 0:64])
                nc.vector.tensor_copy(v_c, q_c[:, :, 256:512]).then_inc(roped, 1)

            def c_stages(g):
                for w in range(C_UNITS):
                    u, stage = 4 + w, C_DVE.get(g - c_base(w))
                    pr = probs_c[w % 2]
                    if stage == "tops":
                        tops(u, 64 ** -0.5, c_at=4 * w)
                    if stage == "recip":
                        recip(u, c=True)
                    if stage == "copy1":
                        copy_pT(pr[:, 1, :], heads_before(u, "C") + 2, 2)
                    if stage == "copy3":
                        copy_pT(pr[:, 3, :], heads_before(u, "C") + 4, 2)
                    if stage == "y":
                        y_out(u, "C")
                    if stage == "lo":
                        y_lo(u, 2 * w, 2, 7)
                for c in range(4):
                    if g == 8 * (c + 1) + 3:
                        biased(C_Q, c, c + 1)
                        for t in range(TT):
                            last = rope(nat[:, t, :].rearrange("p (h d) -> p h d", h=8),
                                        q_c[:, t, :].rearrange("p (h d) -> p h d", h=8), rope_c, t, 8, 64)
                            if t == 0:
                                dve.drain()
                        last.then_inc(roped, 1)
                if g == 3:
                    c_keys()
                if g == 6:
                    dve.wait_ge(kT_done, 5)
                    nc.vector.tensor_copy(kT_c[:, 0:4, :], bank(4, 2).rearrange("p (g s) -> p g s", g=4))
                    nc.vector.tensor_copy(kT_c[:, 4:8, :], bank(6, 2).rearrange("p (g s) -> p g s", g=4)).then_inc(kT_copied, 1)

            for c in range(4):
                for p in range(8):
                    split(C_Q, c, p)
                    c_stages(8 * c + p)
            for p in range(8):
                split(C_OUT0, 0, p)
                c_stages(32 + p)
            for g in range(40, C_LAST):
                c_stages(g)
            for p in range(24):
                split(C_OUT1, 0, p)
                if p == 3:
                    gate_row(2)
                    update(0, 0, C_OUT0.used(0, 0), nth=1)
                if p == 11:
                    update(1, 1, C_OUT1.used(0, 0), nth=1)
                if p == 19:
                    update(2, 0, C_OUT1.used(0, 1), nth=2)
            update(3, 1, C_OUT1.used(0, 2), nth=2)
            columns(SC2[1])
            norm(3)
            norm_out(3)
            ffn(1)
            norm(4)
            dve.drain()
            dve.wait_ge(final_landed, 16)
            for t in range(TT):
                tt(xn[:, t, :], xn[:, t, :], gate[:, :], ALU.mult).then_inc(xn_done, 1)

        @block.tensor
        def _(pe):
            mm = nc.tensor.matmul

            def tr(out, in_):
                return nc.tensor.transpose(out, in_, ident[:, :])

            def pair(ph, i, b, p, slot, hi, lo):
                q = b * ph.pairs + p
                pe.wait_ge(lo_ready, LO_CREDIT + ph.pair(i, q) + 1)
                for k in range(2):
                    kt = 2 * p + k
                    for t in range(TT):
                        out = bank(2 * slot + t)
                        tok = slice(t * P, (t + 1) * P)
                        mm(out, hi[:, kt, tok], w_hi[:, q % PAIRS, k, :], start=(kt == 0), stop=False)
                        mm(out, hi[:, kt, tok], w_lo[:, q % PAIRS, k, :], start=False, stop=False)
                        last = mm(out, lo[:, kt, tok], w_hi[:, q % PAIRS, k, :], start=False,
                                  stop=(kt == 2 * ph.pairs - 1))
                last.then_inc(pair_used, 1)

            def sum_columns(n):
                slot0 = 4 * n % ACC
                pe.wait_ge(ada_step, ADA_CREDIT + 16 * 4 * (n + 1))
                pe.wait_ge(acc_free, ACC_CREDIT + 4 * n)
                for c in range(KT):
                    last = mm(ps[:, 7 * 512 + c:7 * 512 + c + 1], acc[:, slot0 + c // 4, (c % 4) * P:(c % 4 + 1) * P],
                              ones[:, 0:1], start=True, stop=True)
                last.then_inc(mods_summed, 1)

            def spread_gate(n, vec, summed):
                pe.wait_ge(acc_free, ACC_CREDIT + 4 * (summed + 1))
                for c in range(KT):
                    last = mm(ps[:, 4 * 512 + c * P:4 * 512 + (c + 1) * P],
                              mod[:, vec // 6, vec % 6, c:c + 1].broadcast_to([P, P]), ident[:, :], start=True, stop=True)
                last.then_inc(gate_spread, 1)

            def norm(n):
                pe.wait_ge(xn_done, 2 * n + 2)
                for c in range(4):
                    for k in range(4):
                        kt = 4 * c + k
                        for t in range(TT):
                            last = tr(ps[:, kt * SEQ + t * P:kt * SEQ + (t + 1) * P], xn[:, t, kt * P:(kt + 1) * P])
                    last.then_inc(xT_done, 1)

            def q_transposes(i):
                pe.wait_ge(roped, 2 * i + 1)
                for h in range(4):
                    for t in range(TT):
                        last = tr(ps[:, 4 * 512 + h * SEQ + t * P:4 * 512 + h * SEQ + (t + 1) * P],
                                  nat[:, t, h * P:(h + 1) * P])
                last.then_inc(qT_done, 1)

            def k_transposes(i):
                pe.wait_ge(roped, 2 * i + 2)
                for h in range(4):
                    for t in range(TT):
                        last = tr(ps[:, 6 * 512 + h * SEQ + t * P:6 * 512 + h * SEQ + (t + 1) * P],
                                  nat[:, t, h * P:(h + 1) * P])
                last.then_inc(kT_done, 1)

            def scores(q, k, prev_mask):
                for h in range(4):
                    s0 = ps[:, 6 * 512 + h * P:6 * 512 + (h + 1) * P]
                    s1 = 4 * 512 + h * SEQ
                    mm(s0, ident_b[:, :], mask_own[:, :], start=True, stop=False)
                    mm(s0, q(h)[:, 0:P], k(h)[:, 0:P], start=False, stop=True)
                    if prev_mask:
                        mm(ps[:, s1:s1 + P], ident_b[:, :], mask_prev[:, :], start=True, stop=False)
                    mm(ps[:, s1:s1 + P], q(h)[:, P:SEQ], k(h)[:, 0:P], start=not prev_mask, stop=True)
                    mm(ps[:, s1 + P:s1 + SEQ], ident_b[:, :], mask_own[:, :], start=True, stop=False)
                    last = mm(ps[:, s1 + P:s1 + SEQ], q(h)[:, P:SEQ], k(h)[:, P:SEQ], start=False, stop=True)
                last.then_inc(scores_done, 1)

            def p_transposes(src, b):
                for k in range(3):
                    last = tr(bank(b)[:, k * P:(k + 1) * P], src[:, k * P:(k + 1) * P])
                last.then_inc(pT_done, 1)

            def outputs(pTs, v, o0, o1):
                for h, pT in enumerate(pTs):
                    mm(o0(h), pT[:, 0:P], v(h, 0), start=True, stop=True)
                for h, pT in enumerate(pTs):
                    mm(o1(h), pT[:, P:2 * P], v(h, 0), start=True, stop=False)
                    last = mm(o1(h), pT[:, 2 * P:3 * P], v(h, 1), start=False, stop=True)
                last.then_inc(o_done, 1)

            def y_transposes(u, src, n, b):
                pe.wait_ge(y_done, u + 1)
                for k in range(n):
                    for t in range(TT):
                        last = tr(ps[:, b * 512 + k * SEQ + t * P:b * 512 + k * SEQ + (t + 1) * P],
                                  src[:, t, k * P:(k + 1) * P])
                last.then_inc(yT_done, 1)

            pe.wait_ge(s_const, 16 * CONSTS)
            pe.wait_ge(s_setup, 6)
            sum_columns(SH1[0])
            sum_columns(SC1[0])
            pe.wait_ge(acc_free, ACC_CREDIT + 8)
            norm(0)

            def ab_stage(stage, u, kind):
                B = kind == "B"
                if stage == "scores":
                    pe.wait_ge(qT_copied, u + 1)
                    pe.wait_ge(kT_copied, u + 1)
                    scores(lambda h: qT[:, h, :], lambda h: kT[:, h, :], False)
                if stage == "pT01":
                    if B:
                        pe.wait_ge(w_done, u - 1)
                    else:
                        pe.wait_ge(probs_done, u + 1)
                    p_transposes(probs[:, 0, :], 7)
                    p_transposes(probs[:, 2 if B else 1, :], 6)
                if stage == "pT23" and not B:
                    pe.wait_ge(pT_act, 2 * u + 1)
                    p_transposes(probs[:, 2, :], 7)
                    pe.wait_ge(pT_dve, 2 * u + 1)
                    p_transposes(probs[:, 3, :], 6)
                if stage == "out":
                    done = u + 3 if B else 2 * u + 2
                    pe.wait_ge(pT_act, done)
                    pe.wait_ge(pT_dve, done)
                    pe.wait_ge(evacuated, EVAC_CREDIT + 3 * u + 3)
                    d = 256 if B else 128
                    outputs([probs[:, h, :] for h in range(0, 4, 2 if B else 1)],
                            lambda h, t: v_ab[:, t, d * h:d * h + d],
                            lambda h: bank(4)[:, d * h:d * h + d], lambda h: bank(5)[:, d * h:d * h + d])
                if stage == "yT":
                    y_transposes(u, y, 4, 6)

            def ab(i, prev):
                for b in range(3):
                    pe.wait_ge(evacuated, AB_IN.block(i, b) + (2 if b == 0 else 1) if b or prev else 2)
                    for p in range(8):
                        n = 8 * b + p
                        if prev is None and b == 0 and p % 2 == 0:
                            pe.wait_ge(xl_done, p // 2 + 1)
                        if prev is None and b == 1 and p == 0:
                            pe.wait_ge(xl_done, 4)
                        pair(AB_IN, i, b, p, b % 2, xT_hi, xT_lo)
                        if prev:
                            ab_stage(AB_PE.get(n), i - 1, prev)
                        if prev == "B" and n == 17:
                            pe.wait_ge(yTl_done, i)
                            sum_columns(G1[0])
                        if n == 12:
                            q_transposes(i)
                        if n == 20:
                            if prev:
                                pe.wait_ge(yTl_done, i)
                            if prev == "B":
                                pe.wait_ge(acc_free, ACC_CREDIT + 4 * (G1[0] + 1))
                            k_transposes(i)
            ab(0, None)
            repeat(pe, 1, 3, lambda i: ab(i, "A"))
            ab(3, "B")
            def blocks(ph, hi, lo, slot=0, before=None, after=None, tail=None, x_at=None):
                def body(i, first=False):
                    for b in range(ph.blocks):
                        if before:
                            before(i, b)
                        pe.wait_ge(evacuated, ph.block(i, b) + 1)
                        for p in range(ph.pairs):
                            if first and b == 0 and x_at is not None and p % 2 == 0:
                                pe.wait_ge(xl_done, 4 * x_at + p // 2 + 1)
                            if first and b == 0 and tail and p == 6:
                                pe.wait_ge(yTl_done, 4)
                            pair(ph, i, b, p, (slot + b) % 2, hi, lo)
                            if first and b == 0 and tail:
                                ab_stage(tail.get(p), 3, "B")
                            if after and p == 2 and not (first and b == 0):
                                after(ph.blocks * i + b - 1, 1 - b)
                body(0, True)
                repeat(pe, 1, ph.n, body)

            def ab_out_before(i, b):
                if (i, b) == (0, 1):
                    sum_columns(SH2[0])
                    spread_gate(0, G1[0], SH2[0])
            blocks(AB_OUT, hT_hi, hT_lo, slot=1, before=ab_out_before, tail=TAIL_PE)
            pe.wait_ge(gate_copied, 1)
            sum_columns(SC2[0])
            pe.wait_ge(acc_free, ACC_CREDIT + 4 * (SC2[0] + 1))
            norm(1)

            def ffn(layer, n_norm):
                h0 = 22 * layer
                for s, (fin, fout) in enumerate(FFN[layer]):
                    def hid_transposes(j, b):
                        pe.wait_ge(evacuated, EVAC_CREDIT + fin.block0 + j + 1)
                        pe.wait_ge(hTl_done, h0 + j + 1)
                        for k in range(2):
                            for t in range(TT):
                                last = tr(ps[:, (4 + b) * 512 + k * SEQ + t * P:(4 + b) * 512 + k * SEQ + (t + 1) * P],
                                          hid[:, b, t, k * P:(k + 1) * P])
                        last.then_inc(hidT_done, 1)
                    blocks(fin, xT_hi, xT_lo, after=hid_transposes, x_at=n_norm if s == 0 else None)
                    hid_transposes(2 * fin.n - 1, 1)
                    h0 += 2 * fin.n
                    pe.wait_ge(hTl_done, HT_CREDIT + h0)
                    if s == 0:
                        sum_columns(G2[layer])
                    if layer == 0 and s == 1:
                        sum_columns(SC1[1])

                    def before(i, b):
                        if s == 0 and (i, b) == (0, 1):
                            spread_gate(1 + 2 * layer, G2[layer], G2[layer])
                    blocks(fout, hT_hi, hT_lo, before=before)
                    pe.wait_ge(gate_copied, 2 + 2 * layer)
                    if layer == 0:
                        sum_columns((SH1, G1, SH2)[s][1])

            ffn(0, 1)
            norm(2)
            blocks(C_KV, xT_hi, xT_lo, x_at=2)

            def c_stages(g):
                for w in range(C_UNITS):
                    u, c, half, stage = 4 + w, w // 2, w % 2, C_PE.get(g - c_base(w))
                    pr = probs_c[half]
                    if stage == "scores":
                        pe.wait_ge(qT_copied, 5 + w)
                        pe.wait_ge(kT_copied, 5)
                        scores(lambda h: qT[:, 2 * half + h // 2, :], lambda h: kT_c[:, 2 * c + h % 2, :], True)
                    if stage == "pT01":
                        pe.wait_ge(probs_done, u + 1)
                        pe.wait_ge(yTl_done, u)
                        p_transposes(pr[:, 0, :], 7)
                        pe.wait_ge(qT_copied, 4 + min(w + 2, C_UNITS))
                        p_transposes(pr[:, 1, :], 2)
                    if stage == "pT23":
                        pe.wait_ge(pT_act, 2 * u - 1)
                        p_transposes(pr[:, 2, :], 7)
                        pe.wait_ge(pT_dve, 2 * u - 1)
                        p_transposes(pr[:, 3, :], 2)
                    if stage == "out":
                        pe.wait_ge(pT_act, 2 * u)
                        pe.wait_ge(pT_dve, 2 * u)
                        pe.wait_ge(y_done, u)
                        outputs([pr[:, h, :] for h in range(4)], lambda h, t: v_c[:, t, 64 * c:64 * c + 64],
                                lambda h: bank(3)[:, 64 * h:64 * h + 64],
                                lambda h: bank(3)[:, 256 + 64 * h:256 + 64 * h + 64])
                    if stage == "yT":
                        y_transposes(u, y_c, 2, 7)
                for c in range(4):
                    for half, at in ((0, 2), (1, 6)):
                        if g == 8 * (c + 1) + at:
                            pe.wait_ge(roped, 10 + c)
                            for h in range(2):
                                for t in range(TT):
                                    last = tr(bank(2)[:, h * SEQ + t * P:h * SEQ + (t + 1) * P],
                                              nat[:, t, (2 * half + h) * P:(2 * half + h + 1) * P])
                            last.then_inc(qT_done, 1)
                if g == 2:
                    pe.wait_ge(roped, 9)
                    for k in range(8):
                        for t in range(TT):
                            last = tr(ps[:, 4 * 512 + k * SEQ + t * P:4 * 512 + k * SEQ + (t + 1) * P],
                                      k_c[:, t, k // 2, k % 2, :])
                    last.then_inc(kT_done, 1)

            for c in range(5):
                ph, i = (C_Q, c) if c < 4 else (C_OUT0, 0)
                pe.wait_ge(evacuated, ph.block(i, 0) + 2)
                for p in range(8):
                    if c == 4 and p == 5:
                        for g in range(37, C_LAST):
                            c_stages(g)
                        pe.wait_ge(yTl_done, 12)
                    pair(ph, i, 0, p, 0, *((xT_hi, xT_lo) if c < 4 else (hT_hi, hT_lo)))
                    if c < 4 or p < 5:
                        c_stages(8 * c + p)

            def c_out_before(i, b):
                if b == 0:
                    spread_gate(2, G1[1], SH2[1])
            blocks(C_OUT1, hT_hi, hT_lo, slot=1, before=c_out_before)
            pe.wait_ge(gate_copied, 3)
            sum_columns(SC2[1])
            pe.wait_ge(acc_free, ACC_CREDIT + 4 * (SC2[1] + 1))
            norm(3)
            ffn(1, 3)
    return nc


def quads(w, blocks):
    k = w.shape[0]
    t = w.reshape(k // 512, 4, P, blocks, NT)
    return np.ascontiguousarray(t.transpose(3, 0, 2, 1, 4)).reshape(-1, P, 4 * NT)


def rope_table(dim):
    freq = np.float32(10000.0) ** (-np.arange(0, dim, 2, dtype=np.float32) / np.float32(dim))
    angle = np.arange(SEQ, dtype=np.float32)[:, None] * freq[None, :]
    cos, sin = np.cos(angle), np.sin(angle)
    t = np.stack([np.concatenate([cos, cos], -1), np.concatenate([-sin, sin], -1)], 1).astype(np.float32)
    return np.ascontiguousarray(t.reshape(TT, P, 2, dim).transpose(1, 0, 2, 3))


def layouts(i):
    ada_w, ada_b = i["ada_w"], i["ada_b"]
    ab = quads(i["ab_w_in"][0], 12).reshape(12, 4, P, 4 * NT)
    order = [6 * (u // 2) + u % 2 + 2 * b for u in range(4) for b in range(3)]
    swa = quads(i["swa_w_in"][0], 5).reshape(5, 4, P, 4 * NT)
    ffn_in, ffn_out = [], []
    for w_in, w_out in zip(i["ffn_w_in"], i["ffn_w_out"]):
        pairs = w_in.reshape(D, 2, HID // HB, HB).transpose(0, 2, 1, 3).reshape(D, 2 * HID)
        ffn_in.append(quads(pairs, HID // HB))
        at = 0
        for kts in SPLITS:
            ffn_out.append(quads(w_out[at * P:(at + kts) * P], NB))
            at += kts
    key, query = np.arange(P)[None, :], np.arange(P)[:, None]
    masks = np.concatenate([np.where(key <= query, 0.0, MASKED), np.where(key > query, 0.0, MASKED)], 1)
    return {
        "x": i["x"].reshape(SEQ, D),
        "c": i["c"].reshape(KT, P).T,
        "ada": np.concatenate([quads(w, ADA_COLS // NT) for w in ada_w]),
        "ada_bias": ada_b.reshape(2, 6, KT, P).transpose(3, 0, 1, 2),
        "ab_in": ab[order].reshape(-1, P, 4 * NT),
        "ab_out": quads(i["ab_w_out"][0], NB),
        "swa_in": swa[[4, 0, 1, 2, 3]].reshape(-1, P, 4 * NT),
        "swa_out": quads(i["swa_w_out"][0], NB),
        "swa_b_in": i["swa_b_in"].reshape(5, NT)[[4, 0, 1, 2, 3]],
        "swa_b_out": i["swa_b_out"].reshape(NB, NT),
        "ffn_in": np.concatenate(ffn_in),
        "ffn_out": np.concatenate(ffn_out),
        "subln": i["diff_subln"].reshape(256),
        "sinks": i["swa_sinks"].reshape(32),
        "lam": i["diff_lambda"].reshape(512),
        "final_norm": i["final_norm"],
        "ident": np.eye(P, dtype=np.float32),
        "masks": masks.astype(np.float32),
        "rope_ab": rope_table(128),
        "rope_c": rope_table(64),
    }


def kernel(**inputs):
    import concourse.bacc as bacc
    from concourse.bass_utils import run_bass_kernel_spmd as run

    arrays = {k: np.ascontiguousarray(v) for k, v in layouts({k: np.asarray(v) for k, v in inputs.items()}).items()}
    nc = bacc.Bacc("TRN2", target_bir_lowering=False, num_devices=1)
    T = {k: nc.dram_tensor(f"in_{k}", v.shape, F32, kind="ExternalInput").ap() for k, v in arrays.items()}
    T["out"] = nc.dram_tensor("out", (SEQ, D), F32, kind="ExternalOutput").ap()
    for name in ("x", "out"):
        T[name] = T[name].rearrange("(t p) d -> p t d", p=P)
    kernel_program(nc, T)
    r = run(nc, [{f"in_{k}": v for k, v in arrays.items()}], core_ids=[0])
    return r.results[0]["out"].reshape(1, SEQ, D)
```

```python
from contextlib import ExitStack

import numpy as np

import concourse.bass as bass
from concourse import mybir

ALU = mybir.AluOpType
ACT = mybir.ActivationFunctionType
F32 = mybir.dt.float32
F32R = mybir.dt.float32r
BF16 = mybir.dt.bfloat16
AX_X = mybir.AxisListType.X
ds = bass.ds

P = 128
D = 2048
SEQ = 256
TT = SEQ // P
NT = 512
KT = D // P
NB = D // NT
HID = 5632
HB = 256
ADA_COLS = 6 * D
RAW = 4
PAIRS = 4
ADA_RAW = 2
ACC = 8
MOD0_BLOCKS = 8
SPLITS = (16, 16, 12)
LAMBDA_INIT = 0.2
RMS_EPS = 1e-6
SUBLN_EPS = 1e-5
MASKED = -1e30

LO_CREDIT = 2 * RAW
USED_CREDIT = PAIRS
ADA_CREDIT = 4 * ADA_RAW
ACC_CREDIT = ACC
EVAC_CREDIT = 2
HT_CREDIT = 2


class Phase:

    def __init__(self, prev, n, blocks, pairs, ada, src=None, src0=0):
        self.n, self.blocks, self.pairs, self.ada = n, blocks, pairs, ada
        self.quads = blocks * pairs // 2
        self.src, self.src0 = src, src0
        self.quad0 = prev.quad0 + prev.n * prev.quads if prev else 0
        self.block0 = prev.block0 + prev.n * prev.blocks if prev else 0
        self.ada0 = prev.ada0 + prev.n * prev.ada if prev else 0
        self.fills = [len(range(s, self.quads, RAW)) for s in range(RAW)]
        self.fills0 = [a + prev.n * b for a, b in zip(prev.fills0, prev.fills)] if prev else [0] * RAW

    def quad(self, i, t):
        return self.quad0 + i * self.quads + t

    def pair(self, i, p):
        return 2 * self.quad0 + i * (2 * self.quads) + p

    def block(self, i, b):
        return self.block0 + i * self.blocks + b

    def ada_quad(self, i, a):
        return 4 * self.ada0 + i * (4 * self.ada) + a

    def raw_fills(self, i, t):
        s = t % RAW
        return self.fills0[s] + i * self.fills[s] + t // RAW + 1

    def raw_distance(self, t):
        if t >= RAW or self.quads % RAW == 0:
            return RAW
        last = max(u for u in range(self.quads) if u % RAW == t % RAW)
        return self.quads - last + t

    def used(self, i, b):
        return USED_CREDIT + self.pair(i, (b + 1) * self.pairs)

    def ada_fills(self, i, a):
        return 2 * self.ada0 - MOD0_BLOCKS + i * (2 * self.ada) + a // ADA_RAW + 1

    def ada_after(self, t):
        n = 4 * self.ada
        return range(n * t // self.quads, n * (t + 1) // self.quads)

    def ada_steps(self, p):
        n = 16 * self.ada
        return range(n * p // (2 * self.quads), n * (p + 1) // (2 * self.quads))


SH1, SC1, G1, SH2, SC2, G2 = ((v, v + 6) for v in range(6))
SUMMED_AT = (2, 5, 8, 11)

FFN_SUMS = (((None, G2[0]), (SH1[1], SC1[1]), (G1[1], None)), ((None, G2[1]), (None, None), (None, None)))

AB_PE = {0: "scores", 4: "pT01", 6: "pT23", 8: "out", 11: "yT"}
AB_ACT = {4: "exps", 8: "copy0", 10: "copy2", 12: "norm", 15: "hi"}
AB_DVE = {3: "v", 4: "tops", 5: "recip", 8: "copy1", 10: "copy3", 12: "y", 15: "lo"}
TAIL_PE = {0: "scores", 4: "pT01", 6: "out", 9: "yT"}
TAIL_ACT = {4: "exps", 8: "copy0", 10: "norm", 13: "hi"}
TAIL_DVE = {3: "v", 4: "tops", 5: "recip", 8: "copy1", 10: "y", 13: "lo"}
C_PE = {0: "scores", 3: "pT01", 4: "pT23", 6: "out", 7: "yT"}
C_ACT = {4: "exps", 7: "copy0", 8: "copy2", 11: "hi"}
C_DVE = {4: "tops", 6: "recip", 7: "copy1", 8: "copy3", 10: "y", 11: "lo"}
C_UNITS = 8
C_LAST = 8 * 5 + 12

AB_OUT_ORDER = [(b, p) for b in range(2) for p in range(6)] + [(b, p) for b in range(2) for p in (6, 7)] + \
               [(b, p) for b in range(2, 4) for p in range(8)]
AB_OUT_DONE = [AB_OUT_ORDER.index((b, 7)) + 1 for b in range(4)]
AHEAD = PAIRS


def c_base(w):
    return 8 * (w // 2) + 12 + 4 * (w % 2)


def heads_before(u, kind):
    return {"A": 4 * u, "B": 2 * u + 4, "C": 4 * u - 4}[kind]


def kernel_program(nc, T):
    chain = []

    def phase(*a, **k):
        chain.append(Phase(chain[-1] if chain else None, *a, **k))
        return chain[-1]

    MOD0 = phase(MOD0_BLOCKS // 2, 0, 0, 2)
    MOD0.fills = [1] * RAW
    AB_IN = phase(4, 3, 8, 2, src="ab_in")
    AB_OUT = phase(1, 4, 8, 4, src="ab_out")
    FFN = []
    C_KV = C_Q = C_OUT0 = C_OUT1 = None
    for layer in range(2):
        at_in, at_out, runs = layer * (HID // HB) * 4, layer * (HID // P), []
        for s, kts in enumerate(SPLITS):
            in_ada = int(layer == 0 or s == 0)
            out_ada = (2, 2, 1)[s] if layer == 0 else 0
            runs.append((phase(kts // 4, 2, 8, in_ada, src="ffn_in", src0=at_in),
                         phase(2, 2, kts // 2, out_ada, src="ffn_out", src0=at_out)))
            at_in += kts // 2 * 4
            at_out += kts
        FFN.append(runs)
        if layer == 0:
            C_KV = phase(1, 1, 8, 1, src="swa_in")
            C_Q = phase(4, 1, 8, 0, src="swa_in", src0=4)
            C_OUT0 = phase(1, 1, 8, 0, src="swa_out")
            C_OUT1 = phase(1, 3, 8, 2, src="swa_out", src0=4)
    assert chain[-1].ada0 == 48

    with ExitStack() as ctx:
        def sb(name, shape, dt=F32):
            return ctx.enter_context(nc.sbuf_tensor(name, shape, dt))

        def sem(name):
            return ctx.enter_context(nc.semaphore(name))

        x = sb("x", [P, TT, D])
        xT_hi = sb("xT_hi", [P, KT, SEQ], F32R)
        xT_lo = sb("xT_lo", [P, KT, SEQ], F32R)
        hT_hi = sb("hT_hi", [P, KT, SEQ], F32R)
        hT_lo = sb("hT_lo", [P, KT, SEQ], F32R)
        raw = sb("raw", [P, RAW, 4, NT])
        w_hi = sb("w_hi", [P, PAIRS, 2, NT], F32R)
        w_lo = sb("w_lo", [P, PAIRS, 2, NT], F32R)
        ada_raw = sb("ada_raw", [P, ADA_RAW, 4, NT])
        acc = sb("acc", [P, ACC, NT])
        work = sb("work", [P, 4096])
        gate = sb("gate", [P, D])
        ident = sb("ident", [P, P])
        ones = sb("ones", [P, P])
        ident_b = sb("ident_b", [P, P], BF16)
        mask_own = sb("mask_own", [P, P], BF16)
        mask_prev = sb("mask_prev", [P, P], BF16)
        rope_ab = sb("rope_ab", [P, TT, 2, 128])
        rope_c = sb("rope_c", [P, TT, 2, 64])
        subln = sb("subln", [P, 256])
        sinks = sb("sinks", [P, 32])
        cond = sb("cond", [P, KT])
        ada_bias = sb("ada_bias", [P, 2, 6, KT])
        mod = sb("mod", [P, 2, 6, KT])
        ssq = sb("ssq", [P, 8])
        squares = sb("squares", [P, TT, NB])
        rstd = sb("rstd", [P, 8])
        top = sb("top", [P, TT, 4])
        negtop = sb("negtop", [P, TT, 4])
        den = sb("den", [P, TT, 4])
        rden = sb("rden", [P, 2, TT, 4])
        sinkd = sb("sinkd", [P, TT, 4])
        sinke = sb("sinke", [P, TT, 4])
        lam = sb("lam", [P, 4])

        ps = ctx.enter_context(nc.psum_tensor("ps", [P, 8 * 512], F32))

        def bank(b, n=1):
            return ps[:, b * 512:(b + n) * 512]

        nat = work[:, 0:1024].rearrange("p (t n) -> p t n", t=TT)
        qT = work[:, 1024:2048].rearrange("p (h s) -> p h s", h=4)
        y = work[:, 1024:2048].rearrange("p (t n) -> p t n", t=TT)
        kT = work[:, 2048:3072].rearrange("p (h s) -> p h s", h=4)
        v_ab = work[:, 3072:4096].rearrange("p (t n) -> p t n", t=TT)
        q_c = v_ab
        y_c = ada_raw[:, 0, 0, :].rearrange("p (t n) -> p t n", t=TT)
        k_c = work[:, 0:2048].rearrange("p (t g e n) -> p t g e n", t=TT, g=4, e=2)
        bias_c = work[:, 2048:2560]
        probs = gate[:, 0:1536].rearrange("p (h n) -> p h n", h=4)
        probs_c = [probs, ada_raw[:, 1, 1:4, :].rearrange("p a n -> p (a n)").rearrange("p (h n) -> p h n", h=4)]
        rope_t = gate[:, 1536:2048]
        kT_c = acc[:, 4:8, :].rearrange("p a n -> p (a n)").rearrange("p (g s) -> p g s", g=8)
        v_c = ada_raw[:, 1, 0, :].rearrange("p (t n) -> p t n", t=TT)
        silu = work[:, 0:1024].rearrange("p (b t n) -> p b t n", b=2, t=TT)
        hid = work[:, 1024:2048].rearrange("p (b t n) -> p b t n", b=2, t=TT)
        upd = work[:, 2048:3072].rearrange("p (t n) -> p t n", t=TT)
        bias_o = work[:, 3072:4096].rearrange("p (b n) -> p b n", b=2)
        xn = work[:, :].rearrange("p (t n) -> p t n", t=TT)
        squared = xT_lo[:, :, :].rearrange("p k s -> p (k s)").rearrange("p (t n) -> p t n", t=TT)

        s_x = sem("x_landed")
        s_const = sem("constants_landed")
        s_cond = sem("cond_landed")
        raw_landed = [sem(f"raw_landed{s}") for s in range(RAW)]
        ada_landed = [sem(f"ada_landed{s}") for s in range(ADA_RAW)]
        final_landed = sem("final_norm_landed")
        gate_spread = sem("gate_spread")
        gate_copied = sem("gate_copied")
        bias_landed = sem("c_bias_landed")
        bo_landed = [sem(f"c_out_bias_landed{s}") for s in range(2)]
        hi_ready = sem("hi_ready")
        lo_ready = sem("lo_ready")
        pair_used = sem("pair_used")
        evacuated = sem("evacuated")
        s_setup = sem("setup_done")
        s_silu_c = sem("silu_c_done")
        ada_step = sem("ada_step")
        mods_summed = sem("mods_summed")
        acc_free = sem("acc_free")
        ssq_done = sem("ssq_done")
        ms_done = sem("mean_square_done")
        root_done = sem("root_done")
        rstd_done = sem("rstd_done")
        xn_done = sem("xn_done")
        xT_done = sem("xT_done")
        mod_act = sem("modulated_act")
        mod_dve = sem("modulated_dve")
        xh_done = sem("xT_hi_done")
        xl_done = sem("xT_lo_done")
        silu_done = sem("silu_done")
        hidT_done = sem("hidT_done")
        hTh_done = sem("hT_hi_done")
        hTl_done = sem("hT_lo_done")
        roped = sem("roped")
        qT_done = sem("qT_done")
        qT_copied = sem("qT_copied")
        kT_done = sem("kT_done")
        kT_copied = sem("kT_copied")
        scores_done = sem("scores_done")
        top_done = sem("top_done")
        probs_done = sem("probs_done")
        w_done = sem("w_done")
        pT_done = sem("pT_done")
        pT_act = sem("pT_copied_act")
        pT_dve = sem("pT_copied_dve")
        o_done = sem("o_done")
        sub_sq = sem("subln_square_done")
        sub_ms = sem("subln_mean_done")
        sub_root = sem("subln_root_done")
        y_done = sem("y_done")
        yT_done = sem("yT_done")
        yTh_done = sem("yT_hi_done")
        yTl_done = sem("yT_lo_done")
        out_landed = sem("out_landed")

        CONSTS = 8
        block = ctx.enter_context(nc.Block())

        def repeat(eng, lo, hi, body):
            if hi - lo == 1:
                body(lo)
            elif hi > lo:
                with eng.Fori(lo, hi) as i:
                    body(i)

        @block.sync
        def _(sp):
            sp.dma_start(cond[:, :], T["c"]).then_inc(s_cond, 16)

            def ada(ph, i, a):
                q = ph.ada_quad(i, a)
                sp.wait_ge(ada_step, 4 * q + 4)
                sp.dma_start(ada_raw[:, a % ADA_RAW, :, :].rearrange("p a n -> p (a n)"),
                             T["ada"][q]).then_inc(ada_landed[a % ADA_RAW], 16)

            def mod0(i):
                for a in range(8):
                    q = MOD0.ada_quad(i, a)
                    s, ring = (a // 4 * 2 + a % 2, raw) if a % 4 >= 2 else (a % 2, ada_raw)
                    back = 8 if ring is raw else 4
                    if not isinstance(i, int) or q >= back:
                        sp.wait_ge(ada_step, ADA_CREDIT + 4 * (q - back + 2 - a % 2))
                    sp.dma_start(ring[:, s, :, :].rearrange("p a n -> p (a n)"), T["ada"][q])\
                        .then_inc((raw_landed if ring is raw else ada_landed)[s], 16)

            def body(ph, i):
                for t in range(ph.quads):
                    sp.wait_ge(lo_ready, LO_CREDIT + 2 * (ph.quad(i, t) - ph.raw_distance(t) + 1))
                    if ph is AB_IN and t < RAW and isinstance(i, int):
                        sp.wait_ge(ada_step, ADA_CREDIT + 4 * (MOD0.ada_quad(MOD0.n - 1, (3, 3, 7, 7)[t]) + 1))
                    sp.dma_start(raw[:, t % RAW, :, :].rearrange("p a n -> p (a n)"),
                                 T[ph.src][ph.src0 + i * ph.quads + t]).then_inc(raw_landed[t % RAW], 16)
                    for a in ph.ada_after(t):
                        if ph is C_OUT1 and a == 0:
                            sp.wait_ge(yT_done, 12)
                        ada(ph, i, a)

            repeat(sp, 0, 1, mod0)
            sp.dma_start(x[:, :, :], T["x"]).then_inc(s_x, 16)
            repeat(sp, 1, MOD0.n, mod0)
            for n, ph in enumerate(chain[1:]):
                if chain[n].quads % RAW:
                    sp.wait_ge(lo_ready, LO_CREDIT + 2 * ph.quad0)
                repeat(sp, 0, 1, lambda i: body(ph, i))
                repeat(sp, 1, ph.n, lambda i: body(ph, i))

            for n in range(4):
                sp.wait_ge(xn_done, 16 + n + 1)
                half = slice(n % 2 * (D // 2), (n % 2 + 1) * (D // 2))
                sp.dma_start(T["out"][:, n // 2, half], xn[:, n // 2, half]).then_inc(out_landed, 16)
            sp.wait_ge(out_landed, 64)

        @block.gpsimd
        def _(pool):
            pool.sem_inc(lo_ready, LO_CREDIT)
            pool.sem_inc(pair_used, USED_CREDIT)
            pool.sem_inc(ada_step, ADA_CREDIT)
            pool.sem_inc(acc_free, ACC_CREDIT)
            pool.sem_inc(evacuated, EVAC_CREDIT)
            pool.sem_inc(hidT_done, HT_CREDIT)
            pool.sem_inc(hTl_done, HT_CREDIT)
            pool.memset(ones[:, :], 1.0).then_inc(s_setup, 2)
            for dst, name in ((ident[:, :], "ident"), (rope_ab[:, :, :, :], "rope_ab"), (rope_c[:, :, :, :], "rope_c"),
                              (ada_bias[:, :, :, :], "ada_bias"), (work[:, 0:256], "masks")):
                pool.dma_start(dst, T[name]).then_inc(s_const, 16)
            for dst, name in ((subln[:, :], "subln"), (sinks[:, :], "sinks"), (work[:, 256:768], "lam")):
                pool.dma_start(dst, T[name].partition_broadcast(P)).then_inc(s_const, 16)

            for c in range(5):
                if c == 0:
                    pool.wait_ge(xT_done, 12)
                else:
                    pool.wait_ge(evacuated, EVAC_CREDIT + C_KV.block0 + c)
                pool.dma_start(bias_c, T["swa_b_in"][c].partition_broadcast(P)).then_inc(bias_landed, 16)
            pool.wait_ge(yT_done, 12)
            for n in range(NB):
                pool.wait_ge(evacuated, C_OUT0.block0 + n + 1)
                pool.dma_start(bias_o[:, n % 2, :],
                               T["swa_b_out"][n].partition_broadcast(P)).then_inc(bo_landed[n % 2], 16)
            pool.wait_ge(evacuated, EVAC_CREDIT + chain[-1].block0 + 4)
            pool.dma_start(gate[:, :], T["final_norm"].partition_broadcast(P)).then_inc(final_landed, 16)

        @block.scalar
        def _(act):
            def hi(ph, i, p):
                t = p // 2
                if p % 2 == 0:
                    act.wait_ge(raw_landed[t % RAW], 16 * ph.raw_fills(i, t))
                act.wait_ge(pair_used, ph.pair(i, p) + 1)
                nc.scalar.activation(w_hi[:, p % PAIRS, :, :], raw[:, t % RAW, 2 * (p % 2):2 * (p % 2) + 2, :],
                                     ACT.Copy).then_inc(hi_ready, 1)

            def square(j, ready=None):
                if ready is not None:
                    act.wait_ge(evacuated, ready)
                for t in range(TT):
                    last = nc.scalar.activation(squared[:, t, ds(j * NT, NT)], x[:, t, ds(j * NT, NT)], ACT.Square,
                                                accum_out=squares[:, t, ds(j, 1)])
                return last

            def norm(n):
                act.wait_ge(ms_done, n + 1)
                nc.scalar.activation(rstd[:, 2:4], ssq[:, 2:4], ACT.Sqrt).then_inc(root_done, 1)

            def norm_out(n, nxt):
                shift, scale = mod[:, n // 2, 3 * (n % 2), :], mod[:, n // 2, 3 * (n % 2) + 1, :]

                def modulate(c):
                    act.wait_ge(xT_done, 4 * n + c + 1)
                    for k in range(2):
                        kt = 4 * c + k
                        o = ps[:, kt * SEQ:(kt + 1) * SEQ]
                        last = nc.scalar.activation(o, o, ACT.Identity, bias=shift[:, kt:kt + 1],
                                                    scale=scale[:, kt:kt + 1])
                    last.then_inc(mod_act, 1)

                def halve(c):
                    act.wait_ge(mod_act, 4 * n + c + 1)
                    act.wait_ge(mod_dve, 4 * n + c + 1)
                    nc.scalar.activation(xT_hi[:, 4 * c:4 * c + 4, :],
                                         bank(2 * c, 2).rearrange("p (k s) -> p k s", k=4), ACT.Copy).then_inc(xh_done, 1)
                act.wait_ge(acc_free, ACC_CREDIT + 4 * SUMMED_AT[n])
                modulate(0)
                modulate(1)
                halve(0)
                if n == 0:
                    hi(nxt, 0, 0)
                    hi(nxt, 0, 1)
                modulate(2)
                halve(1)
                hi(nxt, 0, 2)
                hi(nxt, 0, 3)
                modulate(3)
                halve(2)
                halve(3)

            def copy_qT(u):
                act.wait_ge(qT_done, u + 1)
                nc.scalar.activation(qT, bank(4, 2).rearrange("p (h s) -> p h s", h=4), ACT.Copy).then_inc(qT_copied, 1)

            def exps(u, scale, pr, c=False):
                act.wait_ge(top_done, u + 1)
                if c:
                    nc.scalar.activation(sinke[:, :, :], sinkd[:, :, :], ACT.Exp)
                for t in range(TT):
                    for h in range(4):
                        src = ps[:, 4 * 512 + 256 * h:4 * 512 + 256 * h + 256] if t else \
                            ps[:, 6 * 512 + 128 * h:6 * 512 + 128 * h + 128]
                        last = nc.scalar.activation(pr[:, h, 128 * t:128 + 256 * t], src, ACT.Exp,
                                                    bias=negtop[:, t, h:h + 1], scale=scale,
                                                    accum_out=den[:, t, h:h + 1])
                last.then_inc(probs_done, 1)

            def copy_pT(dst, done):
                act.wait_ge(pT_done, done)
                nc.scalar.activation(dst, bank(7)[:, 0:384], ACT.Copy).then_inc(pT_act, 1)

            def sub_norm(u):
                act.wait_ge(o_done, u + 1)
                act.wait_ge(y_done, u)
                for t in range(TT):
                    for h in range(2):
                        last = nc.scalar.activation(y[:, t, 256 * h:256 * h + 256],
                                                    ps[:, (4 + t) * 512 + 256 * h:(4 + t) * 512 + 256 * h + 256],
                                                    ACT.Square, accum_out=ssq[:, 4 + 2 * t + h:5 + 2 * t + h])
                last.then_inc(sub_sq, 1)
                act.wait_ge(sub_ms, u - 1)
                nc.scalar.activation(rstd[:, 4:8], ssq[:, 4:8], ACT.Sqrt).then_inc(sub_root, 1)

            def y_hi(u, at, n, b):
                act.wait_ge(yT_done, u + 1)
                nc.scalar.activation(hT_hi[:, ds(at, n), :], ps[:, b * 512:b * 512 + n * SEQ].rearrange("p (k s) -> p k s", k=n),
                                     ACT.Copy).then_inc(yTh_done, 1)

            act.wait_ge(s_cond, 16)
            nc.scalar.activation(cond[:, :], cond[:, :], ACT.Silu).then_inc(s_silu_c, 1)
            act.wait_ge(s_const, 16 * CONSTS)
            act.wait_ge(s_setup, 4)
            nc.scalar.activation(lam[:, 2:4], lam[:, 0:2], ACT.Exp).then_inc(s_setup, 1)
            act.wait_ge(s_x, 16)
            for j in range(NB):
                last = square(j)
            last.then_inc(ssq_done, 1)
            norm(0)
            act.wait_ge(rstd_done, 1)
            for c in range(4):
                for t in range(TT):
                    last = nc.scalar.activation(xn[:, t, c * NT:(c + 1) * NT], x[:, t, c * NT:(c + 1) * NT], ACT.Copy,
                                                scale=rstd[:, t:t + 1])
                last.then_inc(xn_done, 1)
            norm_out(0, AB_IN)

            def ab_stage(stage, u, kind):
                if stage == "exps":
                    exps(u, 128 ** -0.5, probs)
                if stage == "copy0":
                    copy_pT(probs[:, 0, :], heads_before(u, kind) + 1)
                if stage == "copy2" and kind == "A":
                    copy_pT(probs[:, 2, :], heads_before(u, kind) + 3)
                if stage == "norm" and kind == "B":
                    sub_norm(u)
                if stage == "hi":
                    y_hi(u, 4 * u, 4, 6)

            def ab(i, prev):
                for n in range(24):
                    if i or n >= AHEAD:
                        hi(AB_IN, i, n)
                    if prev:
                        ab_stage(AB_ACT.get(n), i - 1, prev)
                    if n == 16:
                        copy_qT(i)
            ab(0, None)
            ab(1, "A")
            ab(2, "A")
            ab(3, "B")
            for n in range(32):
                hi(AB_OUT, 0, n)
                ab_stage(TAIL_ACT.get(n), 3, "B")
                if n in (19, 21, 29):
                    j = (19, 21, 29).index(n)
                    square(j, EVAC_CREDIT + AB_OUT.block0 + j + 1)

            def to_norm(n, ph, nxt):
                hi(nxt, 0, 0)
                hi(nxt, 0, 1)
                square(NB - 1, EVAC_CREDIT + ph.block0 + ph.n * ph.blocks).then_inc(ssq_done, 1)
                norm(n)
                norm_out(n, nxt)

            def ffn(layer):
                h0 = 22 * layer

                def silu_step(ph, h0, j, b):
                    blk = ph.block0 + j
                    act.wait_ge(pair_used, USED_CREDIT + 2 * ph.quad0 + 8 * (j + 1))
                    act.wait_ge(evacuated, blk + 1)
                    nc.scalar.activation(silu[:, b, :, :],
                                         bank(2 * b, 2).rearrange("p (t n) -> p t n", t=TT)[:, :, 0:HB],
                                         ACT.Silu).then_inc(silu_done, 1)

                def hidden_hi(h0, j, b):
                    act.wait_ge(hidT_done, HT_CREDIT + h0 + j + 1)
                    nc.scalar.activation(hT_hi[:, ds(2 * j, 2), :], bank(4 + b).rearrange("p (k s) -> p k s", k=2),
                                         ACT.Copy).then_inc(hTh_done, 1)
                for s, (fin, fout) in enumerate(FFN[layer]):
                    def body(i, first=False):
                        for b in range(2):
                            for p in range(8):
                                if not (first and s == 0 and b == 0 and p < AHEAD):
                                    hi(fin, i, 8 * b + p)
                                if first and b == 0:
                                    continue
                                if p == 3:
                                    silu_step(fin, h0, 2 * i + b - 1, 1 - b)
                                if p == 5:
                                    hidden_hi(h0, 2 * i + b - 1, 1 - b)
                    body(0, True)
                    repeat(act, 1, fin.n, body)

                    def out_body(i, first=False):
                        for b in range(2):
                            for p in range(fout.pairs):
                                hi(fout, i, b * fout.pairs + p)
                                if first and b == 0:
                                    if p == 3:
                                        silu_step(fin, h0, 2 * fin.n - 1, 1)
                                    if p == 5:
                                        hidden_hi(h0, 2 * fin.n - 1, 1)
                                elif s == 2 and p == 5:
                                    square(2 * i + b - 1, EVAC_CREDIT + fout.block0 + 2 * i + b)
                    out_body(0, True)
                    repeat(act, 1, fout.n, out_body)
                    h0 += 2 * fin.n

            to_norm(1, AB_OUT, FFN[0][0][0])
            ffn(0)
            to_norm(2, FFN[0][2][1], C_KV)
            for p in range(AHEAD, 8):
                hi(C_KV, 0, p)

            def c_stages(g):
                for w in range(C_UNITS):
                    u, stage = 4 + w, C_ACT.get(g - c_base(w))
                    pr = probs_c[w % 2]
                    if stage == "exps":
                        exps(u, 64 ** -0.5, pr, c=True)
                    if stage == "copy0":
                        copy_pT(pr[:, 0, :], heads_before(u, "C") + 1)
                    if stage == "copy2":
                        copy_pT(pr[:, 2, :], heads_before(u, "C") + 3)
                    if stage == "hi":
                        y_hi(u, 2 * w, 2, 3)
                for c in range(4):
                    for half, at in ((0, 6), (1, 10)):
                        if g == 8 * (c + 1) + at:
                            act.wait_ge(qT_done, 5 + 2 * c + half)
                            nc.scalar.activation(qT[:, 2 * half:2 * half + 2, :],
                                                 bank(2).rearrange("p (h s) -> p h s", h=2), ACT.Copy).then_inc(qT_copied, 1)
            for c in range(4):
                for p in range(8):
                    hi(C_Q, c, p)
                    c_stages(8 * c + p)
            for p in range(8):
                hi(C_OUT0, 0, p)
                c_stages(32 + p)
            for g in range(40, C_LAST):
                c_stages(g)
            for p in range(24):
                hi(C_OUT1, 0, p)
                if p % 8 == 5:
                    square(p // 8, EVAC_CREDIT + C_OUT0.block0 + p // 8 + 1)
            to_norm(3, C_OUT1, FFN[1][0][0])
            ffn(1)
            square(NB - 1, EVAC_CREDIT + chain[-1].block0 + 4).then_inc(ssq_done, 1)
            norm(4)

        @block.vector
        def _(dve):
            tt = nc.vector.tensor_tensor
            stt = nc.vector.scalar_tensor_tensor

            def lo(ph, i, p):
                dve.wait_ge(hi_ready, ph.pair(i, p) + 1)
                tt(w_lo[:, p % PAIRS, :, :], raw[:, (p // 2) % RAW, 2 * (p % 2):2 * (p % 2) + 2, :],
                   w_hi[:, p % PAIRS, :, :].bitcast(F32), ALU.subtract).then_inc(lo_ready, 1)

            def ada(ph, i, step):
                a, k = step // 4, step % 4
                q = ph.ada_quad(i, a)
                j = i * ph.ada + a // 4
                if k == 0:
                    dve.wait_ge(ada_landed[a % ADA_RAW], 16 * ph.ada_fills(i, a))
                if a % 4 or k:
                    dve.wait_ge(ada_step, ADA_CREDIT + 4 * q + k)
                else:
                    dve.wait_ge(acc_free, ph.ada0 + j + 1)
                slot = (ph.ada0 + j) % ACC if isinstance(j, int) else ph.ada0 % ACC + j
                ada_product(acc[:, ds(slot, 1), :].rearrange("p a n -> p (a n)"),
                            ada_raw[:, a % ADA_RAW, k, :], 4 * (a % 4) + k)

            def ada_product(dst, src, kt):
                if kt == 0:
                    nc.vector.tensor_scalar(dst, src, cond[:, kt:kt + 1], None, ALU.mult).then_inc(ada_step, 1)
                else:
                    stt(out=dst, in0=src, scalar=cond[:, kt:kt + 1], in1=dst, op0=ALU.mult,
                        op1=ALU.add).then_inc(ada_step, 1)

            def mod0(i):
                for a in range(4):
                    for b in range(2):
                        s, landed = (a // 2 * 2 + b, raw_landed) if a % 2 else (b, ada_landed)
                        dve.wait_ge(landed[s], 16 * (i + 1) if a % 2 else 16 * (2 * i + a // 2 + 1))
                    for k in range(4):
                        for b in range(2):
                            s, ring = (a // 2 * 2 + b, raw) if a % 2 else (b, ada_raw)
                            if a or k:
                                dve.wait_ge(ada_step, ADA_CREDIT + 32 * i + 8 * a + 2 * k + b - 1)
                            ada_product(acc[:, ds(4 * b + i, 1), :].rearrange("p a n -> p (a n)"),
                                        ring[:, s, k, :], 4 * a + k)

            def ada_behind(ph, i, p):
                for step in ph.ada_steps(p):
                    ada(ph, i, step)

            def columns(n, h, b=6, order=None):
                layer, vec = n // 6, n % 6
                dve.wait_ge(mods_summed, (2 * n + h if order is None else order) + 1)
                last = nc.vector.tensor_reduce(mod[:, layer, vec, 8 * h:8 * h + 8],
                                               bank(b, 2).rearrange("p (k s) -> p k s", k=8), AX_X, ALU.add)
                if h:
                    dve.drain()
                    last = stt(out=mod[:, layer, vec, :], in0=mod[:, layer, vec, :], scalar=float(vec % 3 == 1),
                               in1=ada_bias[:, layer, vec, :], op0=ALU.add, op1=ALU.add)
                last.then_inc(acc_free, 2)

            def gate_row(n):
                dve.wait_ge(gate_spread, n + 1)
                nc.vector.tensor_copy(gate[:, :], bank(4, 4)).then_inc(gate_copied, 1)
                dve.drain()

            def norm(n, meanwhile=None):
                dve.wait_ge(ssq_done, n + 1)
                nc.vector.tensor_reduce(ssq[:, 0:2], squares[:, :, :], AX_X, ALU.add)
                dve.drain()
                nc.vector.tensor_scalar(ssq[:, 2:4], ssq[:, 0:2], 1.0 / D, RMS_EPS, ALU.mult, ALU.add).then_inc(ms_done, 1)
                if meanwhile:
                    meanwhile()
                dve.wait_ge(root_done, n + 1)
                nc.vector.reciprocal(rstd[:, 0:2], rstd[:, 2:4]).then_inc(rstd_done, 1)
                dve.drain()
                if n in (0, 4):
                    return
                for c in range(4):
                    for t in range(TT):
                        last = nc.vector.tensor_scalar(xn[:, t, c * NT:(c + 1) * NT], x[:, t, c * NT:(c + 1) * NT],
                                                       rstd[:, t:t + 1], None, ALU.mult)
                    last.then_inc(xn_done, 1)

            def norm_out(n, nxt):
                shift, scale = mod[:, n // 2, 3 * (n % 2), :], mod[:, n // 2, 3 * (n % 2) + 1, :]

                def modulate(c):
                    dve.wait_ge(xT_done, 4 * n + c + 1)
                    for k in range(2, 4):
                        kt = 4 * c + k
                        o = ps[:, kt * SEQ:(kt + 1) * SEQ]
                        last = nc.vector.tensor_scalar(o, o, scale[:, kt:kt + 1], shift[:, kt:kt + 1], ALU.mult, ALU.add)
                    last.then_inc(mod_dve, 1)

                def rest(c):
                    dve.wait_ge(xh_done, 4 * n + c + 1)
                    tt(xT_lo[:, 4 * c:4 * c + 4, :], bank(2 * c, 2).rearrange("p (k s) -> p k s", k=4),
                       xT_hi[:, 4 * c:4 * c + 4, :].bitcast(F32), ALU.subtract).then_inc(xl_done, 1)
                dve.drain()
                modulate(0)
                modulate(1)
                rest(0)
                if n == 0:
                    lo(nxt, 0, 0)
                    lo(nxt, 0, 1)
                modulate(2)
                rest(1)
                lo(nxt, 0, 2)
                lo(nxt, 0, 3)
                modulate(3)
                rest(2)
                rest(3)

            def rope(dst, src, table, t, heads, d):
                half = d // 2
                cos = table[:, t, 0, :].unsqueeze(1)
                sin = table[:, t, 1, :].unsqueeze(1)
                tmp = rope_t[:, 0:heads * d].rearrange("p (h d) -> p h d", h=heads)
                tt(tmp[:, :, 0:half], src[:, :, half:d], sin[:, :, 0:half].broadcast_to([P, heads, half]), ALU.mult)
                tt(tmp[:, :, half:d], src[:, :, 0:half], sin[:, :, half:d].broadcast_to([P, heads, half]), ALU.mult)
                tt(dst, src, cos.broadcast_to([P, heads, d]), ALU.mult)
                dve.drain()
                last = tt(dst, dst, tmp, ALU.add)
                return last

            def ab_rope(i, b):
                dve.wait_ge(pair_used, AB_IN.used(i, b))
                if b == 1:
                    dve.wait_ge(qT_done, i + 1)
                for t in range(TT):
                    last = rope(nat[:, t, :].rearrange("p (h d) -> p h d", h=4),
                                bank(2 * ((i + b) % 2) + t).rearrange("p (h d) -> p h d", h=4), rope_ab, t, 4, 128)
                    dve.drain()
                nc.vector.engine_nop().then_inc(evacuated, 1)
                nc.vector.engine_nop().then_inc(roped, 1)

            def ab_v(i):
                dve.wait_ge(pair_used, AB_IN.used(i, 2))
                nc.vector.tensor_copy(v_ab, bank(2 * (i % 2), 2).rearrange("p (t n) -> p t n", t=TT)).then_inc(evacuated, 1)

            def copy_kT(i):
                dve.wait_ge(kT_done, i + 1)
                nc.vector.tensor_copy(kT, bank(6, 2).rearrange("p (h s) -> p h s", h=4)).then_inc(kT_copied, 1)

            def tops(u, scale, c_at=None):
                dve.wait_ge(scores_done, u + 1)
                nc.vector.tensor_reduce(top[:, 0, :], bank(6).rearrange("p (h s) -> p h s", h=4), AX_X, ALU.max)
                nc.vector.tensor_reduce(top[:, 1, :], bank(4, 2).rearrange("p (h s) -> p h s", h=4), AX_X, ALU.max)
                dve.drain()
                if c_at is None:
                    nc.vector.tensor_scalar(negtop[:, :, :], top[:, :, :], -scale, None, ALU.mult).then_inc(top_done, 1)
                    return
                sink = sinks[:, ds(c_at, 4)]
                for t in range(TT):
                    stt(out=top[:, t, :], in0=top[:, t, :], scalar=scale, in1=sink, op0=ALU.mult, op1=ALU.max)
                dve.drain()
                for t in range(TT):
                    tt(sinkd[:, t, :], sink, top[:, t, :], ALU.subtract)
                nc.vector.tensor_scalar(negtop[:, :, :], top[:, :, :], -1.0, None, ALU.mult).then_inc(top_done, 1)

            def recip(u, r=0, c=False):
                dve.wait_ge(probs_done, u + 1)
                if c:
                    tt(den[:, :, :], den[:, :, :], sinke[:, :, :], ALU.add)
                    dve.drain()
                nc.vector.reciprocal(rden[:, r, :, :], den[:, :, :])
                dve.drain()

            def combine(u):
                recip(u)
                for h in range(2):
                    nc.vector.tensor_scalar(rden[:, 0, :, 2 * h + 1], rden[:, 0, :, 2 * h + 1], lam[:, 0:1], None, ALU.mult)
                    for t in range(TT):
                        w = probs[:, 2 * h, 128 * t:128 + 256 * t]
                        nc.vector.tensor_scalar(w, w, rden[:, 0, t, 2 * h:2 * h + 1], None, ALU.mult)
                dve.drain()
                for h in range(2):
                    for t in range(TT):
                        w = probs[:, 2 * h, 128 * t:128 + 256 * t]
                        last = stt(out=w, in0=probs[:, 2 * h + 1, 128 * t:128 + 256 * t],
                                   scalar=rden[:, 0, t, 2 * h + 1:2 * h + 2], in1=w, op0=ALU.mult, op1=ALU.add)
                last.then_inc(w_done, 1)

            def copy_pT(dst, done, b):
                dve.wait_ge(pT_done, done)
                nc.vector.tensor_copy(dst, bank(b)[:, 0:384]).then_inc(pT_dve, 1)

            def y_out(u, kind, r=0):
                dve.wait_ge(o_done, u + 1)
                n, d = (4, 64) if kind == "C" else (4, 128)
                if kind == "B":
                    dve.wait_ge(sub_sq, u - 1)
                    nc.vector.tensor_scalar(ssq[:, 4:8], ssq[:, 4:8], 1.0 / 256, SUBLN_EPS, ALU.mult, ALU.add).then_inc(sub_ms, 1)
                    dve.wait_ge(sub_root, u - 1)
                    nc.vector.reciprocal(rstd[:, 4:8], rstd[:, 4:8])
                    dve.drain()
                    nc.vector.tensor_scalar(rstd[:, 4:8], rstd[:, 4:8], 1.0 - LAMBDA_INIT, None, ALU.mult)
                    dve.drain()
                    for t in range(TT):
                        for h in range(2):
                            last = stt(out=y[:, t, 256 * h:256 * h + 256],
                                       in0=ps[:, (4 + t) * 512 + 256 * h:(4 + t) * 512 + 256 * h + 256],
                                       scalar=rstd[:, 4 + 2 * t + h:5 + 2 * t + h], in1=subln[:, :],
                                       op0=ALU.mult, op1=ALU.mult)
                else:
                    for t in range(TT):
                        src = bank(4 + t) if kind == "A" else bank(3)[:, 256 * t:256 * t + 256]
                        dst = y[:, t, :] if kind == "A" else y_c[:, t, 0:256]
                        last = tt(dst.rearrange("p (h d) -> p h d", h=n), src.rearrange("p (h d) -> p h d", h=n),
                                  rden[:, r, t, :].unsqueeze(2).broadcast_to([P, n, d]), ALU.mult)
                last.then_inc(y_done, 1)

            def y_lo(u, at, n, b):
                dve.wait_ge(yTh_done, u + 1)
                tt(hT_lo[:, ds(at, n), :], ps[:, b * 512:b * 512 + n * SEQ].rearrange("p (k s) -> p k s", k=n),
                   hT_hi[:, ds(at, n), :].bitcast(F32), ALU.subtract).then_inc(yTl_done, 1)

            dve.wait_ge(s_silu_c, 1)
            mod0(0)
            dve.wait_ge(s_const, 16 * CONSTS)
            nc.vector.tensor_copy(ident_b[:, :], ident[:, :])
            nc.vector.tensor_copy(mask_own[:, :], work[:, 0:128])
            nc.vector.tensor_copy(mask_prev[:, :], work[:, 128:256])
            lv = work[:, 256:768].rearrange("p (a b n) -> p a b n", a=2, b=2)
            prod = work[:, 768:1024].rearrange("p (a n) -> p a n", a=2)
            tt(prod, lv[:, :, 0, :], lv[:, :, 1, :], ALU.mult)
            dve.drain()
            nc.vector.tensor_reduce(lam[:, 0:2], prod, AX_X, ALU.add).then_inc(s_setup, 2)
            dve.wait_ge(s_setup, 5)
            tt(lam[:, 0:1], lam[:, 3:4], lam[:, 2:3], ALU.subtract)
            dve.drain()
            nc.vector.tensor_scalar(lam[:, 0:1], lam[:, 0:1], -LAMBDA_INIT, None, ALU.add).then_inc(s_setup, 1)
            repeat(dve, 1, 3, mod0)
            columns(SH1[0], 0, 6, order=0)
            columns(SC1[0], 0, 4, order=1)
            norm(0)
            mod0(3)
            columns(SH1[0], 1, 6, order=2)
            columns(SC1[0], 1, 4, order=3)
            norm_out(0, AB_IN)

            def ab_stage(stage, u, kind):
                B = kind == "B"
                if stage == "v":
                    ab_v(u)
                if stage == "tops":
                    tops(u, 128 ** -0.5)
                if stage == "recip":
                    if B:
                        combine(u)
                    else:
                        recip(u)
                if stage == "copy1":
                    copy_pT(probs[:, 2 if B else 1, :], heads_before(u, kind) + 2, 6)
                if stage == "copy3" and not B:
                    copy_pT(probs[:, 3, :], heads_before(u, kind) + 4, 6)
                if stage == "y":
                    y_out(u, kind)
                if stage == "lo":
                    y_lo(u, 4 * u, 4, 6)

            def ab(i, prev):
                for n in range(24):
                    if i or n >= AHEAD:
                        lo(AB_IN, i, n)
                    if prev:
                        ab_stage(AB_DVE.get(n), i - 1, prev)
                    if prev == "B" and n in (19, 21):
                        columns(G1[0], n // 21)
                    if n == 11:
                        ab_rope(i, 0)
                    if n == 19:
                        ab_rope(i, 1)
                    if n == 23:
                        copy_kT(i)
                    ada_behind(AB_IN, i, n)

            def update(j, b, used, nth=None):
                dve.wait_ge(pair_used, used)
                src = bank(2 * b, 2).rearrange("p (t n) -> p t n", t=TT)
                if nth is not None:
                    dve.wait_ge(bo_landed[j % 2], 16 * nth)
                    tt(upd, src, bias_o[:, j % 2:j % 2 + 1, :].broadcast_to([P, TT, NT]), ALU.add)
                    dve.drain()
                    src = upd
                tt(upd, src, gate[:, ds(j * NT, NT)].unsqueeze(1).broadcast_to([P, TT, NT]), ALU.mult)
                dve.drain()
                xs = x[:, :, ds(j * NT, NT)]
                tt(xs, xs, upd, ALU.add).then_inc(evacuated, 1)

            ab(0, None)
            ab(1, "A")
            ab(2, "A")
            ab(3, "B")
            for n in range(32):
                lo(AB_OUT, 0, n)
                ab_stage(TAIL_DVE.get(n), 3, "B")
                if n == 16:
                    gate_row(0)
                if n in (17, 19, 27):
                    j = (17, 19, 27).index(n)
                    update(j, j % 2, USED_CREDIT + AB_OUT.pair(0, AB_OUT_DONE[j]))
                if n in (18, 23):
                    columns(SH2[0], n // 23)
                ada_behind(AB_OUT, 0, n)

            def to_norm(n, nxt, slot, used, summed, nth=None):
                lo(nxt, 0, 0)
                lo(nxt, 0, 1)
                update(NB - 1, slot, used, nth)
                columns(summed, 0, 4)
                norm(n, lambda: columns(summed, 1, 6))
                norm_out(n, nxt)

            def ffn(layer):
                h0 = 22 * layer

                def gated(ph, h0, j, b):
                    dve.wait_ge(silu_done, h0 + j + 1)
                    dve.wait_ge(hidT_done, h0 + j + 1)
                    tt(hid[:, b, :, :], bank(2 * b, 2).rearrange("p (t n) -> p t n", t=TT)[:, :, HB:2 * HB],
                       silu[:, b, :, :], ALU.mult).then_inc(evacuated, 1)

                def hidden_lo(h0, j, b):
                    dve.wait_ge(hTh_done, h0 + j + 1)
                    tt(hT_lo[:, ds(2 * j, 2), :], bank(4 + b).rearrange("p (k s) -> p k s", k=2),
                       hT_hi[:, ds(2 * j, 2), :].bitcast(F32), ALU.subtract).then_inc(hTl_done, 1)
                for s, (fin, fout) in enumerate(FFN[layer]):
                    summed_in, summed_out = FFN_SUMS[layer][s]

                    def body(i, first=False):
                        for b in range(2):
                            for p in range(8):
                                n = 8 * b + p
                                if not (first and s == 0 and n < AHEAD):
                                    lo(fin, i, n)
                                if p == 3 and not (first and b == 0):
                                    gated(fin, h0, 2 * i + b - 1, 1 - b)
                                if p == 5 and not (first and b == 0):
                                    hidden_lo(h0, 2 * i + b - 1, 1 - b)
                                if first and summed_in and n in (8, 15):
                                    columns(summed_in, n // 15)
                                ada_behind(fin, i, n)

                    def used(j):
                        return USED_CREDIT + 2 * fout.quad0 + fout.pairs * (j + 1)

                    def out_body(i, first=False):
                        for b in range(2):
                            for p in range(fout.pairs):
                                lo(fout, i, b * fout.pairs + p)
                                if first and b == 0:
                                    if p == 3:
                                        gated(fin, h0, 2 * fin.n - 1, 1)
                                    if p == 5:
                                        hidden_lo(h0, 2 * fin.n - 1, 1)
                                    if summed_out and p in (4, 7):
                                        columns(summed_out, p // 7)
                                elif p == 3:
                                    if first and s == 0:
                                        gate_row(1 + 2 * layer)
                                    update(2 * i + b - 1, 1 - b, used(2 * i + b - 1))
                                ada_behind(fout, i, b * fout.pairs + p)
                    body(0, True)
                    repeat(dve, 1, fin.n, body)
                    out_body(0, True)
                    repeat(dve, 1, fout.n, out_body)
                    if s < 2:
                        update(NB - 1, 1, used(NB - 1))
                    h0 += 2 * fin.n

            to_norm(1, FFN[0][0][0], 1, USED_CREDIT + AB_OUT.pair(0, 32), SC2[0])
            ffn(0)
            to_norm(2, C_KV, 1, USED_CREDIT + 2 * C_KV.quad0, SH2[1])
            nc.vector.memset(work[:, 0:2048], 0.0)
            for p in range(8):
                if p >= AHEAD:
                    lo(C_KV, 0, p)
                ada_behind(C_KV, 0, p)

            def biased(ph, i, c):
                dve.wait_ge(pair_used, ph.used(i, 0))
                dve.wait_ge(bias_landed, 16 * (c + 1))
                tt(q_c, bank(2 if c == 0 else 0, 2).rearrange("p (t n) -> p t n", t=TT),
                   bias_c.unsqueeze(1).broadcast_to([P, TT, NT]), ALU.add).then_inc(evacuated, 1)
                dve.drain()

            def c_keys():
                for t in range(TT):
                    rope(k_c[:, t, :, 0, 0:64], q_c[:, t, 0:256].rearrange("p (h d) -> p h d", h=4), rope_c, t, 4, 64)
                    dve.drain()
                    nc.vector.tensor_copy(k_c[:, t, :, 1, 64:128], k_c[:, t, :, 0, 0:64])
                nc.vector.tensor_copy(v_c, q_c[:, :, 256:512]).then_inc(roped, 1)

            def c_stages(g):
                for w in range(C_UNITS):
                    u, stage = 4 + w, C_DVE.get(g - c_base(w))
                    pr = probs_c[w % 2]
                    if stage == "tops":
                        tops(u, 64 ** -0.5, c_at=4 * w)
                    if stage == "recip":
                        recip(u, w % 2, c=True)
                    if stage == "copy1":
                        copy_pT(pr[:, 1, :], heads_before(u, "C") + 2, 2)
                    if stage == "copy3":
                        copy_pT(pr[:, 3, :], heads_before(u, "C") + 4, 2)
                    if stage == "y":
                        y_out(u, "C", w % 2)
                    if stage == "lo":
                        y_lo(u, 2 * w, 2, 3)
                if g == 2:
                    biased(C_KV, 0, 0)
                for c in range(4):
                    if g == 8 * (c + 1) + 2:
                        biased(C_Q, c, c + 1)
                    if g == 8 * (c + 1) + 3:
                        for t in range(TT):
                            last = rope(nat[:, t, :].rearrange("p (h d) -> p h d", h=8),
                                        q_c[:, t, :].rearrange("p (h d) -> p h d", h=8), rope_c, t, 8, 64)
                            if t == 0:
                                dve.drain()
                        last.then_inc(roped, 1)
                if g == 3:
                    c_keys()
                if g == 6:
                    dve.wait_ge(kT_done, 5)
                    nc.vector.tensor_copy(kT_c[:, 0:4, :], bank(4, 2).rearrange("p (g s) -> p g s", g=4))
                    nc.vector.tensor_copy(kT_c[:, 4:8, :], bank(6, 2).rearrange("p (g s) -> p g s", g=4)).then_inc(kT_copied, 1)

            for c in range(4):
                for p in range(8):
                    lo(C_Q, c, p)
                    c_stages(8 * c + p)
            for p in range(8):
                lo(C_OUT0, 0, p)
                c_stages(32 + p)
            for g in range(40, C_LAST):
                c_stages(g)
            for p in range(24):
                lo(C_OUT1, 0, p)
                if p == 3:
                    gate_row(2)
                    update(0, 0, C_OUT0.used(0, 0), nth=1)
                if p == 11:
                    update(1, 1, C_OUT1.used(0, 0), nth=1)
                if p == 19:
                    update(2, 0, C_OUT1.used(0, 1), nth=2)
                ada_behind(C_OUT1, 0, p)
            to_norm(3, FFN[1][0][0], 1, C_OUT1.used(0, 2), SC2[1], nth=2)
            ffn(1)
            update(NB - 1, 1, USED_CREDIT + 2 * (chain[-1].quad0 + chain[-1].n * chain[-1].quads))
            norm(4)
            dve.wait_ge(final_landed, 16)
            for n in range(4):
                t, half = n // 2, slice(n % 2 * (D // 2), (n % 2 + 1) * (D // 2))
                stt(out=xn[:, t, half], in0=x[:, t, half], scalar=rstd[:, t:t + 1], in1=gate[:, half],
                    op0=ALU.mult, op1=ALU.mult).then_inc(xn_done, 1)

        @block.tensor
        def _(pe):
            mm = nc.tensor.matmul

            def tr(out, in_):
                return nc.tensor.transpose(out, in_, ident[:, :])

            def pair(ph, i, b, p, slot, hi, lo, q=None):
                q = b * ph.pairs + p if q is None else q
                pe.wait_ge(lo_ready, LO_CREDIT + ph.pair(i, q) + 1)
                for k in range(2):
                    kt = 2 * p + k
                    for t in range(TT):
                        out = bank(2 * slot + t)
                        tok = slice(t * P, (t + 1) * P)
                        mm(out, hi[:, kt, tok], w_hi[:, q % PAIRS, k, :], start=(kt == 0), stop=False)
                        mm(out, hi[:, kt, tok], w_lo[:, q % PAIRS, k, :], start=False, stop=False)
                        last = mm(out, lo[:, kt, tok], w_hi[:, q % PAIRS, k, :], start=False,
                                  stop=(kt == 2 * ph.pairs - 1))
                last.then_inc(pair_used, 1)

            def sums(n, h, b=6, steps=None, read=None):
                slot0 = 4 * n % ACC + 2 * h
                pe.wait_ge(ada_step, ADA_CREDIT + (16 * (4 * n + 2 * h + 2) if steps is None else steps))
                pe.wait_ge(acc_free, ACC_CREDIT + (4 * n + 2 * h if read is None else read))
                for c in range(8):
                    last = tr(ps[:, b * 512 + c * P:b * 512 + (c + 1) * P],
                              acc[:, slot0 + c // 4, (c % 4) * P:(c % 4 + 1) * P])
                last.then_inc(mods_summed, 1)

            def spread_gate(n, vec, summed):
                pe.wait_ge(acc_free, ACC_CREDIT + 4 * (summed + 1))
                for c in range(KT):
                    last = mm(ps[:, 4 * 512 + c * P:4 * 512 + (c + 1) * P],
                              mod[:, vec // 6, vec % 6, c:c + 1].broadcast_to([P, P]), ident[:, :], start=True, stop=True)
                last.then_inc(gate_spread, 1)

            def norm_blocks(n, blocks):
                for c in blocks:
                    pe.wait_ge(xn_done, 4 * n + c + 1)
                    for k in range(4):
                        kt = 4 * c + k
                        for t in range(TT):
                            last = tr(ps[:, kt * SEQ + t * P:kt * SEQ + (t + 1) * P], xn[:, t, kt * P:(kt + 1) * P])
                    last.then_inc(xT_done, 1)

            def norm(n, summed):
                sums(summed, 0, 4)
                sums(summed, 1, 6, read=4 * summed)
                norm_blocks(n, (0, 1))
                pe.wait_ge(acc_free, ACC_CREDIT + 4 * summed + 2)
                norm_blocks(n, (2,))
                pe.wait_ge(acc_free, ACC_CREDIT + 4 * (summed + 1))
                norm_blocks(n, (3,))

            def q_transposes(i):
                pe.wait_ge(roped, 2 * i + 1)
                for h in range(4):
                    for t in range(TT):
                        last = tr(ps[:, 4 * 512 + h * SEQ + t * P:4 * 512 + h * SEQ + (t + 1) * P],
                                  nat[:, t, h * P:(h + 1) * P])
                last.then_inc(qT_done, 1)

            def k_transposes(i):
                pe.wait_ge(roped, 2 * i + 2)
                for h in range(4):
                    for t in range(TT):
                        last = tr(ps[:, 6 * 512 + h * SEQ + t * P:6 * 512 + h * SEQ + (t + 1) * P],
                                  nat[:, t, h * P:(h + 1) * P])
                last.then_inc(kT_done, 1)

            def scores(q, k, prev_mask):
                for h in range(4):
                    s0 = ps[:, 6 * 512 + h * P:6 * 512 + (h + 1) * P]
                    s1 = 4 * 512 + h * SEQ
                    mm(s0, ident_b[:, :], mask_own[:, :], start=True, stop=False)
                    mm(s0, q(h)[:, 0:P], k(h)[:, 0:P], start=False, stop=True)
                    if prev_mask:
                        mm(ps[:, s1:s1 + P], ident_b[:, :], mask_prev[:, :], start=True, stop=False)
                    mm(ps[:, s1:s1 + P], q(h)[:, P:SEQ], k(h)[:, 0:P], start=not prev_mask, stop=True)
                    mm(ps[:, s1 + P:s1 + SEQ], ident_b[:, :], mask_own[:, :], start=True, stop=False)
                    last = mm(ps[:, s1 + P:s1 + SEQ], q(h)[:, P:SEQ], k(h)[:, P:SEQ], start=False, stop=True)
                last.then_inc(scores_done, 1)

            def p_transposes(src, b):
                for k in range(3):
                    last = tr(bank(b)[:, k * P:(k + 1) * P], src[:, k * P:(k + 1) * P])
                last.then_inc(pT_done, 1)

            def outputs(pTs, v, o0, o1):
                for h, pT in enumerate(pTs):
                    mm(o0(h), pT[:, 0:P], v(h, 0), start=True, stop=True)
                for h, pT in enumerate(pTs):
                    mm(o1(h), pT[:, P:2 * P], v(h, 0), start=True, stop=False)
                    last = mm(o1(h), pT[:, 2 * P:3 * P], v(h, 1), start=False, stop=True)
                last.then_inc(o_done, 1)

            def y_transposes(u, src, n, b):
                pe.wait_ge(y_done, u + 1)
                for k in range(n):
                    for t in range(TT):
                        last = tr(ps[:, b * 512 + k * SEQ + t * P:b * 512 + k * SEQ + (t + 1) * P],
                                  src[:, t, k * P:(k + 1) * P])
                last.then_inc(yT_done, 1)

            pe.wait_ge(s_const, 16 * CONSTS)
            pe.wait_ge(s_setup, 6)
            sums(SH1[0], 0, 6, steps=64, read=0)
            sums(SC1[0], 0, 4, steps=64, read=0)
            norm_blocks(0, (0, 1))
            sums(SH1[0], 1, 6, steps=128, read=2)
            sums(SC1[0], 1, 4, steps=128, read=4)
            pe.wait_ge(acc_free, ACC_CREDIT + 8)
            norm_blocks(0, (2, 3))

            def ab_stage(stage, u, kind):
                B = kind == "B"
                if stage == "scores":
                    pe.wait_ge(qT_copied, u + 1)
                    pe.wait_ge(kT_copied, u + 1)
                    scores(lambda h: qT[:, h, :], lambda h: kT[:, h, :], False)
                if stage == "pT01":
                    if B:
                        pe.wait_ge(w_done, u - 1)
                    else:
                        pe.wait_ge(probs_done, u + 1)
                    p_transposes(probs[:, 0, :], 7)
                    p_transposes(probs[:, 2 if B else 1, :], 6)
                if stage == "pT23" and not B:
                    pe.wait_ge(pT_act, 2 * u + 1)
                    p_transposes(probs[:, 2, :], 7)
                    pe.wait_ge(pT_dve, 2 * u + 1)
                    p_transposes(probs[:, 3, :], 6)
                if stage == "out":
                    done = u + 3 if B else 2 * u + 2
                    pe.wait_ge(pT_act, done)
                    pe.wait_ge(pT_dve, done)
                    pe.wait_ge(evacuated, EVAC_CREDIT + 3 * u + 3)
                    d = 256 if B else 128
                    outputs([probs[:, h, :] for h in range(0, 4, 2 if B else 1)],
                            lambda h, t: v_ab[:, t, d * h:d * h + d],
                            lambda h: bank(4)[:, d * h:d * h + d], lambda h: bank(5)[:, d * h:d * h + d])
                if stage == "yT":
                    y_transposes(u, y, 4, 6)

            def ab(i, prev):
                for b in range(3):
                    pe.wait_ge(evacuated, AB_IN.block(i, b) + 1)
                    for p in range(8):
                        n = 8 * b + p
                        if prev is None and b == 0 and p % 2 == 0:
                            pe.wait_ge(xl_done, p // 2 + 1)
                        pair(AB_IN, i, b, p, (i + b) % 2, xT_hi, xT_lo)
                        if prev:
                            ab_stage(AB_PE.get(n), i - 1, prev)
                        if prev == "B" and n in (15, 17):
                            pe.wait_ge(yTl_done, i)
                            sums(G1[0], n // 17)
                        if n == 12:
                            q_transposes(i)
                        if n == (20 if prev == "B" else 19):
                            if prev:
                                pe.wait_ge(yTl_done, i)
                            if prev == "B":
                                pe.wait_ge(acc_free, ACC_CREDIT + 4 * (G1[0] + 1))
                            k_transposes(i)
            ab(0, None)
            ab(1, "A")
            ab(2, "A")
            ab(3, "B")

            for n, (b, p) in enumerate(AB_OUT_ORDER):
                if p == 0:
                    pe.wait_ge(evacuated, AB_OUT.block(0, b) + 1)
                if n == 12:
                    pe.wait_ge(yTl_done, 4)
                pair(AB_OUT, 0, b, p, b % 2, hT_hi, hT_lo, q=n)
                ab_stage(TAIL_PE.get(n), 3, "B")
                if n == 12:
                    spread_gate(0, G1[0], G1[0])
                if n == 14:
                    pe.wait_ge(gate_copied, 1)
                if n in (14, 19):
                    sums(SH2[0], n // 19)
            norm(1, SC2[0])

            def blocks(ph, hi, lo, slot=0, x_at=None, before=None, behind=None):
                def body(i, first=False):
                    for b in range(ph.blocks):
                        pe.wait_ge(evacuated, ph.block(i, b) + 1)
                        for p in range(ph.pairs):
                            if first and b == 0 and x_at is not None and p % 2 == 0:
                                pe.wait_ge(xl_done, 4 * x_at + max(p // 2, slot) + 1)
                            if before:
                                before(i, b, p, first)
                            pair(ph, i, b, p, (slot + b) % 2, hi, lo)
                            if behind:
                                behind(i, b, p, first)
                body(0, True)
                repeat(pe, 1, ph.n, body)

            def ffn(layer, n_norm):
                h0 = 22 * layer
                for s, (fin, fout) in enumerate(FFN[layer]):
                    summed_in, summed_out = FFN_SUMS[layer][s]

                    def hid_transposes(j, b):
                        pe.wait_ge(evacuated, EVAC_CREDIT + fin.block0 + j + 1)
                        pe.wait_ge(hTl_done, h0 + j + 1)
                        for k in range(2):
                            for t in range(TT):
                                last = tr(ps[:, (4 + b) * 512 + k * SEQ + t * P:(4 + b) * 512 + k * SEQ + (t + 1) * P],
                                          hid[:, b, t, k * P:(k + 1) * P])
                        last.then_inc(hidT_done, 1)

                    def behind_in(i, b, p, first):
                        if p == 2 and not (first and b == 0):
                            hid_transposes(2 * i + b - 1, 1 - b)
                        if first and summed_in and (b, p) in ((0, 4), (1, 3)):
                            sums(summed_in, b)

                    def before_out(i, b, p, first):
                        if first and b == 0 and p == fout.pairs - 1:
                            pe.wait_ge(hTl_done, HT_CREDIT + h0 + 2 * fin.n)

                    def behind_out(i, b, p, first):
                        if first and b == 0:
                            if p == 2:
                                hid_transposes(2 * fin.n - 1, 1)
                            if summed_out and p in (0, 3):
                                sums(summed_out, p // 3)
                            if s == 0 and p == fout.pairs - 1:
                                spread_gate(1 + 2 * layer, G2[layer], G2[layer])
                    blocks(fin, xT_hi, xT_lo, x_at=n_norm if s == 0 else None, behind=behind_in)
                    blocks(fout, hT_hi, hT_lo, before=before_out, behind=behind_out)
                    pe.wait_ge(gate_copied, 2 + 2 * layer)
                    h0 += 2 * fin.n

            ffn(0, 1)
            norm(2, SH2[1])
            blocks(C_KV, xT_hi, xT_lo, slot=1, x_at=2)

            def c_stages(g):
                for w in range(C_UNITS):
                    u, c, half, stage = 4 + w, w // 2, w % 2, C_PE.get(g - c_base(w))
                    pr = probs_c[half]
                    if stage == "scores":
                        pe.wait_ge(qT_copied, 5 + w)
                        pe.wait_ge(kT_copied, 5)
                        scores(lambda h: qT[:, 2 * half + h // 2, :], lambda h: kT_c[:, 2 * c + h % 2, :], True)
                    if stage == "pT01":
                        pe.wait_ge(probs_done, u + 1)
                        p_transposes(pr[:, 0, :], 7)
                        pe.wait_ge(qT_copied, 4 + min(w + 2, C_UNITS))
                        p_transposes(pr[:, 1, :], 2)
                    if stage == "pT23":
                        pe.wait_ge(pT_act, 2 * u - 1)
                        p_transposes(pr[:, 2, :], 7)
                        pe.wait_ge(pT_dve, 2 * u - 1)
                        p_transposes(pr[:, 3, :], 2)
                    if stage == "out":
                        pe.wait_ge(pT_act, 2 * u)
                        pe.wait_ge(pT_dve, 2 * u)
                        pe.wait_ge(yTl_done, u)
                        outputs([pr[:, h, :] for h in range(4)], lambda h, t: v_c[:, t, 64 * c:64 * c + 64],
                                lambda h: bank(3)[:, 64 * h:64 * h + 64],
                                lambda h: bank(3)[:, 256 + 64 * h:256 + 64 * h + 64])
                    if stage == "yT":
                        y_transposes(u, y_c, 2, 3)
                for c in range(4):
                    for half, at in ((0, 2), (1, 6)):
                        if g == 8 * (c + 1) + at:
                            pe.wait_ge(roped, 10 + c)
                            if c:
                                pe.wait_ge(pT_dve, 2 * (4 + 2 * c - 2 + half))
                            for h in range(2):
                                for t in range(TT):
                                    last = tr(bank(2)[:, h * SEQ + t * P:h * SEQ + (t + 1) * P],
                                              nat[:, t, (2 * half + h) * P:(2 * half + h + 1) * P])
                            last.then_inc(qT_done, 1)
                if g == 2:
                    pe.wait_ge(roped, 9)
                    for k in range(8):
                        for t in range(TT):
                            last = tr(ps[:, 4 * 512 + k * SEQ + t * P:4 * 512 + k * SEQ + (t + 1) * P],
                                      k_c[:, t, k // 2, k % 2, :])
                    last.then_inc(kT_done, 1)

            for c in range(5):
                ph, i = (C_Q, c) if c < 4 else (C_OUT0, 0)
                pe.wait_ge(evacuated, ph.block(i, 0) + (2 if c else 1))
                for p in range(8):
                    if c == 4 and p == 5:
                        for g in range(37, C_LAST):
                            c_stages(g)
                    if c == 4:
                        pe.wait_ge(yTl_done, 5 + p)
                    pair(ph, i, 0, p, 0, *((xT_hi, xT_lo) if c < 4 else (hT_hi, hT_lo)))
                    if c < 4 or p < 5:
                        c_stages(8 * c + p)

            spread_gate(2, G1[1], SH2[1])
            blocks(C_OUT1, hT_hi, hT_lo, slot=1)
            pe.wait_ge(gate_copied, 3)
            norm(3, SC2[1])
            ffn(1, 3)
    return nc


def quads(w, blocks):
    k = w.shape[0]
    t = w.reshape(k // 512, 4, P, blocks, NT)
    return np.ascontiguousarray(t.transpose(3, 0, 2, 1, 4)).reshape(-1, P, 4 * NT)


def rope_table(dim):
    freq = np.float32(10000.0) ** (-np.arange(0, dim, 2, dtype=np.float32) / np.float32(dim))
    angle = np.arange(SEQ, dtype=np.float32)[:, None] * freq[None, :]
    cos, sin = np.cos(angle), np.sin(angle)
    t = np.stack([np.concatenate([cos, cos], -1), np.concatenate([-sin, sin], -1)], 1).astype(np.float32)
    return np.ascontiguousarray(t.reshape(TT, P, 2, dim).transpose(1, 0, 2, 3))


def layouts(i):
    ada_w, ada_b = i["ada_w"], i["ada_b"]
    ab = quads(i["ab_w_in"][0], 12).reshape(12, 4, P, 4 * NT)
    order = [6 * (u // 2) + u % 2 + 2 * b for u in range(4) for b in range(3)]
    swa = quads(i["swa_w_in"][0], 5).reshape(5, 4, P, 4 * NT)
    ffn_in, ffn_out = [], []
    for w_in, w_out in zip(i["ffn_w_in"], i["ffn_w_out"]):
        pairs = w_in.reshape(D, 2, HID // HB, HB).transpose(0, 2, 1, 3).reshape(D, 2 * HID)
        ffn_in.append(quads(pairs, HID // HB))
        at = 0
        for kts in SPLITS:
            ffn_out.append(quads(w_out[at * P:(at + kts) * P], NB))
            at += kts
    key, query = np.arange(P)[None, :], np.arange(P)[:, None]
    masks = np.concatenate([np.where(key <= query, 0.0, MASKED), np.where(key > query, 0.0, MASKED)], 1)
    ada = np.concatenate([quads(w, ADA_COLS // NT) for w in ada_w])
    ada[:32] = ada[:32].reshape(2, 4, 4, P, 4 * NT).transpose(1, 2, 0, 3, 4).reshape(32, P, 4 * NT)
    ab_out = quads(i["ab_w_out"][0], NB)[[4 * b + p // 2 for b, p in AB_OUT_ORDER if p % 2 == 0]]
    return {
        "x": i["x"].reshape(SEQ, D),
        "c": i["c"].reshape(KT, P).T,
        "ada": ada,
        "ada_bias": ada_b.reshape(2, 6, KT, P).transpose(3, 0, 1, 2),
        "ab_in": ab[order].reshape(-1, P, 4 * NT),
        "ab_out": ab_out,
        "swa_in": swa[[4, 0, 1, 2, 3]].reshape(-1, P, 4 * NT),
        "swa_out": quads(i["swa_w_out"][0], NB),
        "swa_b_in": i["swa_b_in"].reshape(5, NT)[[4, 0, 1, 2, 3]],
        "swa_b_out": i["swa_b_out"].reshape(NB, NT),
        "ffn_in": np.concatenate(ffn_in),
        "ffn_out": np.concatenate(ffn_out),
        "subln": i["diff_subln"].reshape(256),
        "sinks": i["swa_sinks"].reshape(32),
        "lam": i["diff_lambda"].reshape(512),
        "final_norm": i["final_norm"],
        "ident": np.eye(P, dtype=np.float32),
        "masks": masks.astype(np.float32),
        "rope_ab": rope_table(128),
        "rope_c": rope_table(64),
    }


def kernel(**inputs):
    import concourse.bacc as bacc
    from concourse.bass_utils import run_bass_kernel_spmd as run

    arrays = {k: np.ascontiguousarray(v) for k, v in layouts({k: np.asarray(v) for k, v in inputs.items()}).items()}
    nc = bacc.Bacc("TRN2", target_bir_lowering=False, num_devices=1)
    T = {k: nc.dram_tensor(f"in_{k}", v.shape, F32, kind="ExternalInput").ap() for k, v in arrays.items()}
    T["out"] = nc.dram_tensor("out", (SEQ, D), F32, kind="ExternalOutput").ap()
    for name in ("x", "out"):
        T[name] = T[name].rearrange("(t p) d -> p t d", p=P)
    kernel_program(nc, T)
    r = run(nc, [{f"in_{k}": v for k, v in arrays.items()}], core_ids=[0])
    return r.results[0]["out"].reshape(1, SEQ, D)
```
